# Optimizing a Trainium2 kernel written in Bass

```python
import jax, jax.numpy as jnp
from jax import lax
import numpy as np

D_MODEL = 1024
BATCH = 1
SEQ = 512
DEPTH = 1
DEC_BATCH = 8
DEC_SEQ = 8
PAST_LEN = 1024
PAGE_SIZE = 128

HEAD_DIM = 64
MIX_WIDTH = D_MODEL
GROUP_WIDTH = MIX_WIDTH // 4
N_GROUP_HEADS = GROUP_WIDTH // HEAD_DIM
H_RWKV = N_GROUP_HEADS
H_FOX = N_GROUP_HEADS
H_MOBA = N_GROUP_HEADS
H_SB = N_GROUP_HEADS
H_ATT = H_FOX + H_MOBA + H_SB
RWKV_DECAY_RANK = 64
RWKV_A_RANK = 64
RWKV_GATE_RANK = 128
N_RWKV_COLS = 3 * GROUP_WIDTH + RWKV_DECAY_RANK + RWKV_A_RANK + RWKV_GATE_RANK
N_IN = N_RWKV_COLS + 3 * H_ATT * HEAD_DIM + H_FOX
D_FF = 4 * D_MODEL
MOBA_BLOCK = 256
MOBA_TOPK = 3
Q_BLOCK = 128
MOBA_Q_BLOCK = 64
RMS_EPS = 1e-6
RWKV_GN_EPS = 64e-5
RWKV_DECAY_OFFSET = 0.5
FORGET_BIAS = 3.0
POOL_NUM = 5
POOL_DEN = 4

kernel_name = 'hybrid_rwkv7_fox_moba_stickbreaking_step'

def rms_norm(x, g):
    xf = x.astype(jnp.float32)
    y = xf * lax.rsqrt(jnp.mean(xf * xf, axis=-1, keepdims=True) + RMS_EPS)
    return (y * g.astype(jnp.float32)).astype(x.dtype)

def _blocks(a, blk):
    b, t = a.shape[:2]
    return jnp.moveaxis(a.reshape((b, t // blk, blk) + a.shape[2:]), 1, 0)

def _unblocks(a):
    a = jnp.moveaxis(a, 0, 1)
    return a.reshape((a.shape[0], -1) + a.shape[3:])

def _sweep(fn, blk, arrays, q_pos):
    t = q_pos.shape[0]
    blk = min(blk, t)
    xs = tuple(_blocks(a, blk) for a in arrays) + (q_pos.reshape(t // blk, blk),)
    return _unblocks(lax.map(fn, xs))

def rwkv7_group(p, shift0, s0, mu, w0, w_up, a0, a_up, g_up, k_k, k_a, r_k, gn_w, gn_b):
    b, t, _ = p.shape
    f32 = jnp.float32
    prev = jnp.concatenate([shift0[:, None, :].astype(p.dtype), p[:, :-1]], axis=1)
    xm = p + (prev - p) * mu
    gw = GROUP_WIDTH
    cuts = [gw, 2 * gw, 3 * gw, 3 * gw + RWKV_DECAY_RANK, 3 * gw + RWKV_DECAY_RANK + RWKV_A_RANK]
    r, k, v, xw, xa, xg = jnp.split(xm, cuts, axis=-1)
    w_log = -jax.nn.softplus(-(w0 + jnp.tanh(xw) @ w_up)) - RWKV_DECAY_OFFSET
    decay = jnp.exp(-jnp.exp(w_log.astype(f32)))
    a = jax.nn.sigmoid(a0 + xa @ a_up)
    g = jax.nn.sigmoid(xg) @ g_up
    heads = lambda z: z.reshape(b, t, H_RWKV, HEAD_DIM).astype(f32)
    kk = heads(k * k_k)
    kk = kk * lax.rsqrt(jnp.maximum(jnp.sum(kk * kk, axis=-1, keepdims=True), 1e-24))
    k = k * (1.0 + (a - 1.0) * k_a)
    rh, wh, kh, vh, ah = heads(r), heads(decay), heads(k), heads(v), heads(a)

    def step(s, inp):
        r_t, w_t, k_t, v_t, kk_t, a_t = inp
        sa = jnp.einsum('bhij,bhj->bhi', s, -kk_t)
        s = (s * w_t[:, :, None, :] + sa[..., None] * (kk_t * a_t)[:, :, None, :]
             + v_t[..., None] * k_t[:, :, None, :])
        return s, jnp.einsum('bhij,bhj->bhi', s, r_t)

    xs = tuple(jnp.moveaxis(z, 1, 0) for z in (rh, wh, kh, vh, kk, ah))
    s_fin, y = lax.scan(step, s0.astype(f32), xs)
    y = jnp.moveaxis(y, 0, 1)
    mean = jnp.mean(y, axis=-1, keepdims=True)
    var = jnp.mean(jnp.square(y - mean), axis=-1, keepdims=True)
    y = ((y - mean) * lax.rsqrt(var + RWKV_GN_EPS)).reshape(b, t, gw) * gn_w + gn_b
    bonus = (jnp.sum(rh * kh * r_k, axis=-1, keepdims=True) * vh).reshape(b, t, gw)
    out = ((y + bonus) * g).astype(p.dtype)
    return out, p[:, -1], s_fin.astype(s0.dtype)

def fox_attention(q, k, v, c, blk):
    t, l = q.shape[1], k.shape[1]
    k_pos = jnp.arange(l)
    q_pos = l - t + jnp.arange(t)
    cq = c[:, l - t:]
    ck = jnp.moveaxis(c, 1, 2)
    scale = HEAD_DIM ** -0.5

    def one(args):
        qb, cqb, pb = args
        s = jnp.einsum('bqhd,bkhd->bhqk', qb, k).astype(jnp.float32) * scale
        s = s + jnp.moveaxis(cqb, 1, 2)[..., None] - ck[:, :, None, :]
        s = jnp.where(k_pos[None, :] <= pb[:, None], s, -jnp.inf)
        pr = jax.nn.softmax(s, axis=-1)
        return jnp.einsum('bhqk,bkhd->bqhd', pr.astype(v.dtype), v)

    return _sweep(one, blk, (q, cq), q_pos)

def stick_breaking_attention(q, k, v, blk):
    t, l = q.shape[1], k.shape[1]
    k_pos = jnp.arange(l)
    q_pos = l - t + jnp.arange(t)
    scale = HEAD_DIM ** -0.5

    def one(args):
        qb, pb = args
        z = jnp.einsum('bqhd,bkhd->bhqk', qb, k).astype(jnp.float32) * scale
        m = k_pos[None, :] < pb[:, None]
        log_keep = jnp.where(m, jax.nn.log_sigmoid(-z), 0.0)
        cum = jnp.cumsum(log_keep, axis=-1)
        log_a = jax.nn.log_sigmoid(z) + cum[..., -1:] - cum
        att = jnp.where(m, jnp.exp(log_a), 0.0)
        return jnp.einsum('bhqk,bkhd->bqhd', att.astype(v.dtype), v)

    return _sweep(one, blk, (q,), q_pos)

def moba_attention(q, k, v, blk):
    b, t, h, d = q.shape
    l = k.shape[1]
    n_blocks = max(-(-l // MOBA_BLOCK), MOBA_TOPK)
    pad = n_blocks * MOBA_BLOCK - l
    kp = jnp.pad(k, ((0, 0), (0, pad), (0, 0), (0, 0)))
    vp = jnp.pad(v, ((0, 0), (0, pad), (0, 0), (0, 0)))
    kb = jnp.transpose(kp.reshape(b, n_blocks, MOBA_BLOCK, h, d), (0, 3, 1, 2, 4))
    vb = jnp.transpose(vp.reshape(b, n_blocks, MOBA_BLOCK, h, d), (0, 3, 1, 2, 4))
    k_mean = jnp.mean(kb.astype(jnp.float32), axis=3)
    q_pos = l - t + jnp.arange(t)
    b_idx = jnp.arange(b)[:, None, None, None]
    h_idx = jnp.arange(h)[None, :, None, None]
    blk_range = jnp.arange(n_blocks)
    in_block = jnp.arange(MOBA_BLOCK)
    scale = HEAD_DIM ** -0.5

    def one(args):
        qb, pb = args
        nq = pb.shape[0]
        own = pb // MOBA_BLOCK
        gate = jnp.einsum('bqhd,bhnd->bhqn', qb.astype(jnp.float32), k_mean)
        gate = jnp.where(blk_range[None, :] < own[:, None], gate, -jnp.inf)
        _, top = lax.top_k(gate, MOBA_TOPK)
        top_ok = top < own[:, None]
        own_b = jnp.broadcast_to(own[:, None], (b, h, nq, 1))
        sel = jnp.concatenate([top, own_b], axis=-1)
        ok = jnp.concatenate([top_ok, jnp.ones(own_b.shape, bool)], axis=-1)
        kg = kb[b_idx, h_idx, sel]
        vg = vb[b_idx, h_idx, sel]
        key_pos = sel[..., None] * MOBA_BLOCK + in_block
        mask = ok[..., None] & (key_pos <= pb[:, None, None])
        s = jnp.einsum('bqhd,bhqnkd->bhqnk', qb, kg).astype(jnp.float32) * scale
        s = jnp.where(mask, s, -jnp.inf)
        pr = jax.nn.softmax(s, axis=(-2, -1))
        return jnp.einsum('bhqnk,bhqnkd->bqhd', pr.astype(vg.dtype), vg)

    return _sweep(one, blk, (q,), q_pos)

def decoder_layer(x, shift0, s0, kv_past, logf_past, lw):
    b, t, _ = x.shape
    a_w = H_ATT * HEAD_DIM
    n_qk = H_FOX + H_MOBA
    h = rms_norm(x, lw['attn_norm'])
    proj = h @ lw['w_in']
    p_rwkv = proj[..., :N_RWKV_COLS]
    q, k, v = (proj[..., N_RWKV_COLS + i * a_w:N_RWKV_COLS + (i + 1) * a_w].reshape(b, t, H_ATT, HEAD_DIM)
               for i in range(3))
    f_logit = proj[..., N_RWKV_COLS + 3 * a_w:]
    q = jnp.concatenate([rms_norm(q[:, :, :n_qk], lw['q_norm']), q[:, :, n_qk:]], axis=2)
    k = jnp.concatenate([rms_norm(k[:, :, :n_qk], lw['k_norm']), k[:, :, n_qk:]], axis=2)
    log_f = jax.nn.log_sigmoid((f_logit + lw['b_forget']).astype(jnp.float32))
    kv_new = jnp.stack([k, v], axis=2)
    if kv_past is None:
        kv_all, logf_all = kv_new, log_f
    else:
        kv_all = jnp.concatenate([kv_past.astype(kv_new.dtype), kv_new], axis=1)
        logf_all = jnp.concatenate([logf_past.astype(jnp.float32), log_f], axis=1)
    c_all = jnp.cumsum(logf_all, axis=1)
    k_all, v_all = kv_all[:, :, 0], kv_all[:, :, 1]

    y_rwkv, shift_new, s_new = rwkv7_group(
        p_rwkv, shift0, s0, lw['rwkv_mu'], lw['rwkv_w0'], lw['rwkv_w_up'], lw['rwkv_a0'],
        lw['rwkv_a_up'], lw['rwkv_g_up'], lw['rwkv_k_k'], lw['rwkv_k_a'], lw['rwkv_r_k'],
        lw['rwkv_gn_w'], lw['rwkv_gn_b'])
    fs, ms, ss = slice(0, H_FOX), slice(H_FOX, n_qk), slice(n_qk, H_ATT)
    y_fox = fox_attention(q[:, :, fs], k_all[:, :, fs], v_all[:, :, fs], c_all, Q_BLOCK)
    y_moba = moba_attention(q[:, :, ms], k_all[:, :, ms], v_all[:, :, ms], MOBA_Q_BLOCK)
    y_sb = stick_breaking_attention(q[:, :, ss], k_all[:, :, ss], v_all[:, :, ss], Q_BLOCK)
    y_att = jnp.concatenate([y_fox, y_moba, y_sb], axis=2).reshape(b, t, H_ATT * HEAD_DIM)
    mix = jnp.concatenate([y_rwkv, y_att.astype(y_rwkv.dtype)], axis=-1)
    x = x + mix @ lw['w_out']
    h2 = rms_norm(x, lw['mlp_norm'])
    x = x + jnp.square(jax.nn.relu(h2 @ lw['w_mlp_up'])) @ lw['w_mlp_down']
    return x, kv_new, log_f.astype(x.dtype), s_new, shift_new

def setup_inputs(seed: int = 0) -> dict:
    key = jax.random.key(seed)
    ks = jax.random.split(key, 32)
    f32 = jnp.float32

    def nrm(k, shape, scale=1.0):
        return scale * jax.random.normal(k, shape, f32)

    n_pages = PAST_LEN // PAGE_SIZE
    n_pool = (POOL_NUM * DEC_BATCH * n_pages + POOL_DEN - 1) // POOL_DEN
    L, GW = DEPTH, GROUP_WIDTH
    page_table = jax.random.permutation(ks[6], n_pool)[:DEC_BATCH * n_pages]
    page_table = page_table.reshape(DEC_BATCH, n_pages).astype(jnp.int32)
    return {
        'x_prompt': nrm(ks[0], (BATCH, SEQ, D_MODEL)),
        'x_sample': nrm(ks[1], (DEC_BATCH, DEC_SEQ, D_MODEL)),
        'cache_kv': nrm(ks[2], (DEPTH, n_pool, PAGE_SIZE, 2, H_ATT, HEAD_DIM)),
        'cache_logf': jax.nn.log_sigmoid(FORGET_BIAS + nrm(ks[3], (DEPTH, n_pool, PAGE_SIZE, H_FOX))),
        'state_wkv': nrm(ks[4], (DEPTH, DEC_BATCH, H_RWKV, HEAD_DIM, HEAD_DIM), 0.3),
        'state_shift': nrm(ks[5], (DEPTH, DEC_BATCH, N_RWKV_COLS)),
        'page_table': page_table,
        'attn_norm': 1.0 + nrm(ks[7], (L, D_MODEL), 0.05),
        'w_in': nrm(ks[8], (L, D_MODEL, N_IN), D_MODEL ** -0.5),
        'rwkv_mu': jax.random.uniform(ks[9], (L, N_RWKV_COLS), f32),
        'rwkv_w0': nrm(ks[10], (L, GW), 0.5) - 0.5,
        'rwkv_w_up': nrm(ks[11], (L, RWKV_DECAY_RANK, GW), RWKV_DECAY_RANK ** -0.5),
        'rwkv_a0': nrm(ks[12], (L, GW), 0.1),
        'rwkv_a_up': nrm(ks[13], (L, RWKV_A_RANK, GW), RWKV_A_RANK ** -0.5),
        'rwkv_g_up': nrm(ks[14], (L, RWKV_GATE_RANK, GW), RWKV_GATE_RANK ** -0.5),
        'rwkv_k_k': 0.85 + nrm(ks[15], (L, GW), 0.05),
        'rwkv_k_a': 1.0 + nrm(ks[16], (L, GW), 0.05),
        'rwkv_r_k': nrm(ks[17], (L, H_RWKV, HEAD_DIM), 0.1),
        'rwkv_gn_w': 1.0 + nrm(ks[18], (L, GW), 0.05),
        'rwkv_gn_b': nrm(ks[19], (L, GW), 0.02),
        'q_norm': 1.0 + nrm(ks[20], (L, H_FOX + H_MOBA, HEAD_DIM), 0.05),
        'k_norm': 1.0 + nrm(ks[21], (L, H_FOX + H_MOBA, HEAD_DIM), 0.05),
        'b_forget': FORGET_BIAS + nrm(ks[22], (L, H_FOX), 0.1),
        'w_out': nrm(ks[23], (L, MIX_WIDTH, D_MODEL), MIX_WIDTH ** -0.5),
        'mlp_norm': 1.0 + nrm(ks[24], (L, D_MODEL), 0.05),
        'w_mlp_up': nrm(ks[25], (L, D_MODEL, D_FF), D_MODEL ** -0.5),
        'w_mlp_down': nrm(ks[26], (L, D_FF, D_MODEL), D_FF ** -0.5),
    }

def reference(x_prompt, x_sample, cache_kv, cache_logf, state_wkv, state_shift, page_table,
              attn_norm, w_in, rwkv_mu, rwkv_w0, rwkv_w_up, rwkv_a0, rwkv_a_up, rwkv_g_up,
              rwkv_k_k, rwkv_k_a, rwkv_r_k, rwkv_gn_w, rwkv_gn_b, q_norm, k_norm, b_forget,
              w_out, mlp_norm, w_mlp_up, w_mlp_down):
    yp, ys = x_prompt, x_sample
    bp, db = x_prompt.shape[0], x_sample.shape[0]
    kvp_l, kvs_l, lfp_l, lfs_l, sp_l, ss_l, shp_l, shs_l = [], [], [], [], [], [], [], []
    for l in range(DEPTH):
        lw = dict(attn_norm=attn_norm[l], w_in=w_in[l], rwkv_mu=rwkv_mu[l], rwkv_w0=rwkv_w0[l],
                  rwkv_w_up=rwkv_w_up[l], rwkv_a0=rwkv_a0[l], rwkv_a_up=rwkv_a_up[l],
                  rwkv_g_up=rwkv_g_up[l], rwkv_k_k=rwkv_k_k[l], rwkv_k_a=rwkv_k_a[l],
                  rwkv_r_k=rwkv_r_k[l], rwkv_gn_w=rwkv_gn_w[l], rwkv_gn_b=rwkv_gn_b[l],
                  q_norm=q_norm[l], k_norm=k_norm[l], b_forget=b_forget[l], w_out=w_out[l],
                  mlp_norm=mlp_norm[l], w_mlp_up=w_mlp_up[l], w_mlp_down=w_mlp_down[l])
        shift0 = jnp.zeros((bp, N_RWKV_COLS), yp.dtype)
        s0 = jnp.zeros((bp, H_RWKV, HEAD_DIM, HEAD_DIM), yp.dtype)
        yp, kvp, lfp, sp, shp = decoder_layer(yp, shift0, s0, None, None, lw)
        past_kv = cache_kv[l, page_table].reshape(db, -1, 2, H_ATT, HEAD_DIM)
        past_lf = cache_logf[l, page_table].reshape(db, -1, H_FOX)
        ys, kvs, lfs, ss, shs = decoder_layer(ys, state_shift[l], state_wkv[l], past_kv, past_lf, lw)
        kvp_l.append(kvp); kvs_l.append(kvs); lfp_l.append(lfp); lfs_l.append(lfs)
        sp_l.append(sp); ss_l.append(ss); shp_l.append(shp); shs_l.append(shs)
    kv_prompt, kv_sample = jnp.stack(kvp_l), jnp.stack(kvs_l)
    logf_prompt, logf_sample = jnp.stack(lfp_l), jnp.stack(lfs_l)
    wkv_prompt, wkv_sample = jnp.stack(sp_l), jnp.stack(ss_l)
    shift_prompt, shift_sample = jnp.stack(shp_l), jnp.stack(shs_l)
    return (yp, ys, kv_prompt, kv_sample, logf_prompt, logf_sample, wkv_prompt, wkv_sample, shift_prompt, shift_sample)


_drawn_inputs = setup_inputs


def setup_inputs(seed=0):
    import zlib

    import numpy as np

    out = dict(_drawn_inputs(seed))
    spreads = {}
    factors = {'cache_logf': 3.333, 'rwkv_k_k': 4.77, 'rwkv_gn_w': 3.926, 'rwkv_gn_b': 8.0, 'q_norm': 8.0}
    for name, (base, spread) in spreads.items():
        noise = np.random.default_rng([zlib.crc32(name.encode()), seed]).standard_normal(out[name].shape)
        drawn = base * np.exp(spread * noise) if base else spread * noise
        out[name] = __import__('jax').numpy.asarray(drawn.astype(out[name].dtype))
    for name, factor in factors.items():
        out[name] = (out[name] * factor).astype(out[name].dtype)
    return out
```

```python
from contextlib import ExitStack

import numpy as np
import concourse.bass as bass
from concourse import mybir

F32 = mybir.dt.float32
I32 = mybir.dt.int32
ALU = mybir.AluOpType
ACT = mybir.ActivationFunctionType
AX = mybir.AxisListType

D = 1024
SEQ, DB, DT = 512, 8, 8
NS = DB * DT
T = SEQ + NS
PAST, PAGE = 1024, 128
NPG = PAST // PAGE
HD = 64
H_ATT = 12
AW = H_ATT * HD
N_RW = 1024
DFF = 4 * D
KT = D // 128
CH = 64
NCH = T // CH
TILES = [(i * 128, 128) for i in range(4)] + [(SEQ, NS)]
NEG = -1e30
SP_MAX = 30.0
RMS_EPS = 1e-6
GN_EPS = 64e-5
DECAY = -float(np.exp(-0.5))
KEYS = PAST + NS
BLK = 256
NBLK = PAST // BLK

C_AN, C_MN, C_MU, C_W0, C_A0, C_KK, C_KA, C_RK, C_GW, C_GB, C_QN = 0, 8, 16, 24, 26, 28, 30, 32, 34, 36, 38
C_BM = 44
C_BF = 52
N_PRM = 56
K_ID, K_ONE, K_CAU, K_STR, K_ID64 = 0, 128, 256, 384, 512
N_CST = 576
R_SU, R_IU, R_LEV, R_L1, R_L1T, R_BM = 0, 576, 1152, 1472, 1536, 1600
N_RC = 2112
S_MASK, S_HOT, S_HB, S_LM, S_IOTA, S_QBD = 0, 512, 1024, 1280, 1344, 1348
N_SC = S_QBD


def constants():
    p = np.arange(128)
    cst = np.zeros((128, N_CST), np.float32)
    cst[:, K_ID:K_ID + 128] = np.eye(128)
    cst[:, K_ONE:K_ONE + 128] = (p[:, None] // 64 == p[None, :] // 64)
    cst[:, K_CAU:K_CAU + 128] = np.where(p[None, :] <= p[:, None], 0, NEG)
    cst[:, K_STR:K_STR + 128] = np.where(p[None, :] < p[:, None], 0, NEG)
    q = p % 64
    t = np.arange(64)
    cst[:, K_ID64:K_ID64 + 64] = (q[:, None] == t[None, :])
    rc = np.zeros((128, N_RC), np.float32)
    same = q[:, None] // DT == t[None, :] // DT
    for at, keep in ((R_SU, q[:, None] < t[None, :]), (R_IU, q[:, None] <= t[None, :])):
        for c in range(NCH):
            rc[:, at + c * CH:at + (c + 1) * CH] = keep if c < NCH - 1 else keep & same
    def level(a, b, m):
        return (a // (2 * m) == b // (2 * m)) & (a // m % 2 == 1) & (b // m % 2 == 0)
    for n, m in enumerate((2, 4, 8, 16, 32)):
        rc[:, R_LEV + n * 64:R_LEV + (n + 1) * 64] = level(t[None, :], q[:, None], m)
    rc[:, R_L1:R_L1 + 64] = level(q[:, None], t[None, :], 1)
    rc[:, R_L1T:R_L1T + 64] = level(t[None, :], q[:, None], 1)
    for b in range(DB):
        rc[:, R_BM + b * 64:R_BM + (b + 1) * 64] = (t // DT == b)
    sc = np.zeros((128, N_SC), np.float32)
    r = p % DT
    strict = (p // 32 == 2)
    for b in range(DB):
        own = t[None, :] // DT == b
        s = t[None, :] % DT
        ok = own & np.where(strict[:, None], s < r[:, None], s <= r[:, None])
        sc[:, S_MASK + b * 64:S_MASK + (b + 1) * 64] = np.where(ok, 0, NEG)
    for h in range(4):
        sc[h, S_HOT + h * 128:S_HOT + (h + 1) * 128] = -1
    for b in range(DB):
        for h in range(4):
            sc[4 * b + h, S_HB + 32 * b + 8 * h:S_HB + 32 * b + 8 * h + 8] = -1
            sc[4 * b + h, S_LM:S_LM + 64] = (t // DT == b)
    sc[:, S_IOTA:S_IOTA + 4] = np.arange(1, 5)
    return cst, rc, sc


def build(nc, d, o):
    ctx = ExitStack()
    with ctx:
        def sb(name, shape, dt=F32):
            return ctx.enter_context(nc.sbuf_tensor(name, shape, dt))

        def sem(name):
            return ctx.enter_context(nc.semaphore(name))

        cst = sb("cst", [128, N_CST])
        rc = sb("rc", [128, N_RC])
        prm = sb("prm", [128, N_PRM])
        NW = 3
        W = sb("W", [128, NW, 4096])
        HM = sb("HM", [128, 8, T])
        QK = sb("QK", [128, 12, T])
        VQ = sb("VQ", [128, 7680])
        AR = sb("AR", [128, 16, 2 * T])
        small = sb("small", [128, 264])
        pt_sb = sb("pt_sb", [1, DB * NPG], I32)
        PS = ctx.enter_context(nc.psum_tensor("PS", [128, 8 * 512], F32))

        ident = cst[:, K_ID:K_ID + 128]
        ones_head = cst[:, K_ONE:K_ONE + 128]
        hT = HM
        mixT = HM
        qT, kT = QK[:, 0:6, :], QK[:, 6:12, :]
        h2T = QK[:, 0:8, :]
        xin = VQ[:, 0:5 * D].rearrange("p (t c) -> p t c", t=5)
        V = VQ[:, 0:5 * AW].rearrange("p (t c) -> p t c", t=5)
        ring = VQ[:, 5 * AW:].rearrange("p (g t c) -> p g t c", g=2, t=5)
        x2 = xin

        def slot(n):
            if n >= 16:
                return HM[:, 2 * (n - 16):2 * (n - 16) + 2, :]
            return AR[:, n, :].rearrange("p (a t) -> p a t", a=2)

        def chunked(n):
            return slot(n).rearrange("p a (c s) -> p a c s", s=CH)

        ARf = AR[:, :, :].rearrange("p a c -> p (a c)")
        pT = ARf[:, 0:8 * T].rearrange("p (a t) -> p a t", a=8)
        xm = ARf[:, 8 * T:16 * T].rearrange("p (a t) -> p a t", a=8)
        xs = ARf[:, 16 * T:16 * T + 5 * D].rearrange("p (t c) -> p t c", t=5)
        reset = AR[:, 14, 0:T]
        knorm = AR[:, 14, T:T + 512]
        sqtmp = AR[:, 15, :].rearrange("p (g c) -> p g c", g=3)
        lora = AR[:, 12, 0:512]
        shift_sb = AR[0:9, 13, 0:N_RW]
        shift0 = small[:, 128:192].rearrange("p (m b) -> p m b", m=8)
        ssq = small[:, 0:5]
        rstd = small[:, 5:10]
        eps = small[:, 10:11]
        gneps = small[:, 11:12]
        omka = small[:, 12:14]
        qss = small[:, 16:46].rearrange("p (t h) -> p t h", t=5)
        qrs = small[:, 46:76].rearrange("p (t h) -> p t h", t=5)
        logf = small[:, 76:96]
        ftmp = small[:, 96:116]
        gq = small[:, 116:122]
        nmax = small[:, 192:200]
        rsum = small[:, 200:208]
        rinv = small[:, 208:216]
        gate = small[:, 216:220]
        gsel = small[:, 220:224]
        gmin = small[:, 224:226]
        onec = small[:, 226:227]
        lfx = small[0:NS, 228:260]
        pc = sb("pc", [128, 2, 16])

        X4 = VQ[:, 5 * AW:]
        S0 = X4[:, 0:1024].rearrange("p (a b i) -> p a b i", a=2, b=DB)
        hexp = X4[:, 1024:2048].rearrange("p (a b i) -> p a b i", a=2, b=DB)
        uexp = X4[:, 2048:3072].rearrange("p (a b i) -> p a b i", a=2, b=DB)
        sfin = X4[:, 3648:3776].rearrange("p (a i) -> p a i", a=2)

        NKR = 4
        Kr = ARf[:, 0:NKR * AW].rearrange("p (r c) -> p r c", r=NKR)
        Vr = ARf[:, NKR * AW:(NKR + NPG) * AW].rearrange("p (r c) -> p r c", r=NPG)
        at0 = (NKR + NPG) * AW
        Call = X4[0:32, 2048:2048 + KEYS]
        cT = X4[0:4, 3136:3136 + SEQ]
        qbd = rc[:, S_QBD:S_QBD + 384].rearrange("p (g c q) -> p g c q", g=2, c=6)
        cb = ARf[:, at0:at0 + 4 * SEQ].rearrange("p (h k) -> p h k", h=4)
        NP_ = 3
        Pp = ARf[:, at0 + 2048:at0 + 2048 + NP_ * 512].rearrange("p (r k) -> p r k", r=NP_)
        PTp = ARf[:, at0 + 3584:at0 + 3584 + 2 * 512].rearrange("p (r k) -> p r k", r=2)
        Ya = ARf[:, at0 + 4608:at0 + 4608 + 2 * AW].rearrange("p (r k) -> p r k", r=2)
        T1p = ARf[:, at0 + 6144:at0 + 6144 + 1024].rearrange("p (r k) -> p r k", r=2)
        T2p = ARf[:, at0 + 7168:at0 + 7168 + 520]
        KTb = ARf[:, at0:at0 + 3072].rearrange("p (g c k) -> p g c k", g=2, c=6)
        Z = ARf[0:96, at0 + 3072:at0 + 3072 + 2 * KEYS].rearrange("p (g k) -> p g k", g=2)
        T1 = ARf[0:96, at0 + 5248:at0 + 5248 + KEYS]
        T2 = ARf[0:96, at0 + 6336:at0 + 6336 + KEYS + 4]
        PTs = ARf[:, at0 + 7500:at0 + 7500 + 9 * 96].rearrange("p (k r) -> p k r", k=9)
        assert at0 + 7500 + 9 * 96 <= 16 * 2 * T

        uT = ARf[:, :].rearrange("p (f t) -> p f t", f=32)

        in_const = sem("in_const")
        in_resid = sem("in_resid")
        in_rc = sem("in_rc")
        in_sc = sem("in_sc")
        in_s0 = sem("in_s0")
        in_lf = sem("in_lf")
        in_lora = sem("in_lora")
        in_kn = sem("in_kn")
        dn_used = sem("dn_used")
        y_stored = sem("y_stored")
        stored = sem("stored")
        v_step = sem("v_step")
        a_step = sem("a_step")
        init = sem("init")
        squares = sem("squares")
        std_ready = sem("std_ready")
        xs_ready = sem("xs_ready")
        xT_ps = sem("xT_ps")
        hT_ready = sem("hT_ready")
        p_ps = sem("p_ps")
        p_ready = sem("p_ready")
        qkv_ps = sem("qkv_ps")
        qkv_ev = sem("qkv_ev")
        sq_ready = sem("sq_ready")
        sq_used = sem("sq_used")
        qstd_ready = sem("qstd_ready")
        qk_normed = sem("qk_normed")
        tr_ps = sem("tr_ps")
        tr_ev = sem("tr_ev")
        k_out = sem("k_out")
        xm_ready = sem("xm_ready")
        shift_ps = sem("shift_ps")
        shift_ev = sem("shift_ev")
        shift_out = sem("shift_out")
        lact = sem("lact")
        lora_ps = sem("lora_ps")
        lora_ev = sem("lora_ev")
        kksq_ready = sem("kksq_ready")
        hs_ps = sem("hs_ps")
        hs_ev = sem("hs_ev")
        kkstd_ready = sem("kkstd_ready")
        bonus_in = sem("bonus_in")
        exp_in = sem("exp_in")
        exp_out = sem("exp_out")
        ops_ready = sem("ops_ready")
        c_ps = sem("c_ps")
        c_ev = sem("c_ev")
        ltm_ready = sem("ltm_ready")
        masked_ready = sem("masked_ready")
        logf_in = sem("logf_in")
        logf_a = sem("logf_a")
        logf_ready = sem("logf_ready")
        gnstd_ready = sem("gnstd_ready")
        rw_done = sem("rw_done")
        s1_ready = sem("s1_ready")
        lt_ps = sem("lt_ps")
        lfx_ready = sem("lfx_ready")
        cT_ready = sem("cT_ready")
        lfn_ready = sem("lfn_ready")
        cb_ps = sem("cb_ps")
        cb_ready = sem("cb_ready")
        s_ps = sem("s_ps")
        a_in = sem("a_in")
        a_mid = sem("a_mid")
        sb_in = sem("sb_in")
        p_out = sem("p_out")
        pt_ps = sem("pt_ps")
        pt_ev = sem("pt_ev")
        pv_ps = sem("pv_ps")
        pv_ev = sem("pv_ev")
        mt_ps = sem("mt_ps")
        mt_ev = sem("mt_ev")
        kt_ps = sem("kt_ps")
        kt_ev = sem("kt_ev")
        sg_ps = sem("sg_ps")
        ss_ps = sem("ss_ps")
        qbd_ready = sem("qbd_ready")
        call_ready = sem("call_ready")
        z_abs = sem("z_abs")
        z_ln = sem("z_ln")
        z_max = sem("z_max")
        z_sb = sem("z_sb")
        z_exp = sem("z_exp")
        pn_ready = sem("pn_ready")
        spt_ps = sem("spt_ps")
        spt_ev = sem("spt_ev")
        spv_ps = sem("spv_ps")
        spv_ev = sem("spv_ev")
        o_ps = sem("o_ps")
        o_ev = sem("o_ev")
        x2_ssq = sem("x2_ssq")
        x2_std = sem("x2_std")
        x2s_ready = sem("x2s_ready")
        h2_ps = sem("h2_ps")
        h2_ready = sem("h2_ready")
        u_ps = sem("u_ps")
        u_ev = sem("u_ev")
        u_sq = sem("u_sq")
        y_ps = sem("y_ps")
        y_ready = sem("y_ready")
        in_x = [sem(f"in_x{i}") for i in range(5)]
        in_w = [sem(f"in_w{i}") for i in range(NW)]
        in_k = [sem(f"in_k{i}") for i in range(NKR)]
        in_v = [sem(f"in_v{i}") for i in range(NPG)]
        w_in = d["w_in"][0].rearrange("(k p) c -> p k c", p=128)
        w_out = d["w_out"][0].rearrange("(k p) c -> p k c", p=128)
        w_up = d["w_mlp_up"][0].rearrange("(k p) c -> p k c", p=128)
        w_dn = d["w_mlp_down"][0].rearrange("(k p) c -> p k c", p=128)
        QC = 384
        QW = [QC] * 5 + [QC + 4]
        pieces = [w_in[:, :, g * 512:(g + 1) * 512] for g in range(2)]
        pieces += [w_in[:, :, N_RW + g * QC:N_RW + g * QC + QW[g]] for g in range(6)]
        P_OUT = len(pieces)
        pieces += [w_out[:, :, g * 512:(g + 1) * 512] for g in range(2)]
        P_UP = len(pieces)
        pieces += [w_up[:, :, g * 512:(g + 1) * 512] for g in range(8)]
        P_DN = len(pieces)
        pieces += [w_dn[:, g * 8:(g + 1) * 8, n * 512:(n + 1) * 512] for n in range(2) for g in range(4)]

        def wview(n):
            cols = pieces[n].shape[2]
            return W[:, n % NW, 0:8 * cols].rearrange("p (k c) -> p k c", k=8)

        def w_wait(eng, n):
            eng.wait_ge(in_w[n % NW], 16 * (n // NW + 1))

        def used(n):
            if n < 2:
                return p_ps, 4 * (n + 1)
            if n < P_OUT:
                return qkv_ps, 5 * (n - 1)
            if n < P_UP:
                return o_ps, 5 * (n - P_OUT + 1)
            if n < P_DN:
                return u_ps, 4 * (n - P_UP + 1)
            half, g = divmod(n - P_DN, 4)
            return (dn_used, 3 * half + g + 1) if g < 3 else (y_ps, 5 * (half + 1))

        def xrows(i):
            t0, nr = TILES[i]
            return d["x_prompt"][0, t0:t0 + nr, :] if i < 4 else d["x_sample"].rearrange("b t c -> (b t) c")

        def orows(name, i, c0, c1):
            t0, nr = TILES[i]
            if i < 4:
                return o[name + "_prompt"][t0:t0 + nr, c0:c1]
            return o[name + "_sample"][:, c0:c1]

        def pair(n, width=2 * 288):
            return PS[:, n * 1024:(n + 1) * 1024].rearrange("p (a t) -> p a t", a=2)[:, :, 0:width // 2]

        def halves(ap):
            return ap.rearrange("p (a t) -> p a t", a=2)

        STEPS = [(k, a) for k in ("LT", "L", "ArbT", "LkT", "ArkT", "Vt", "KQt", "BEt", "KEt") for a in (0, 1)]
        for lev in range(5):
            STEPS += [(f"{k}{lev}", a) for k in (("W", "dX", "dXT") if lev < 4 else ("W", "dXT")) for a in (0, 1)]
        STEPS += [(k, a) for k in ("T1", "HT", "H", "G", "MT", "N") for a in (0, 1)]
        STEPS += [(f"seq{c}", 0) for c in range(1, 8)]
        STEPS += [(k, a) for k in ("U", "Y", "SS", "GM", "GV") for a in (0, 1)]
        AT = {s: n for n, s in enumerate(STEPS)}

        UNITS = [(qt, h) for qt in range(4) for h in range(H_ATT)]
        NU = len(UNITS)

        def is_sb(u):
            return 0 <= u < NU and UNITS[u][1] >= 8

        block = ctx.enter_context(nc.Block())

        @block.sync
        def _(sp):
            for i, (t0, nr) in enumerate(TILES):
                sp.dma_start(xin[0:nr, i, :], xrows(i)).then_inc(in_x[i], 16)
            sp.dma_start(cst[:, :], d["cst"]).then_inc(in_const, 16)
            sp.dma_start(prm[:, :], d["prm"]).then_inc(in_const, 16)
            sp.dma_start(small[:, 128:192], d["shift0"]).then_inc(in_const, 16)
            sp.dma_start(pt_sb[:, :], d["page_table"].rearrange("(o b) n -> o (b n)", o=1)).then_inc(in_const, 16)
            sp.dma_start(rc[:, :], d["rc"]).then_inc(in_rc, 16)

            def load_w(n):
                if n >= NW:
                    sp.wait_ge(*used(n - NW))
                sp.dma_start(wview(n), pieces[n]).then_inc(in_w[n % NW], 16)

            for n in range(NW):
                load_w(n)
            sp.wait_ge(xT_ps, 5)
            sp.dma_start(lora[:, 0:256], d["lora_wa"]).then_inc(in_lora, 16)
            sp.dma_start(lora[:, 256:512], d["rwkv_g_up"][0]).then_inc(in_lora, 16)
            sp.dma_start(knorm, d["k_norm"].rearrange("l h d -> l (h d)").to_broadcast([128, 512])).then_inc(in_kn, 16)
            for n in range(NW, P_OUT + NW):
                load_w(n)
            sp.wait_ge(tr_ps, 20)
            sp.wait_ge(k_out, 16 * 10)
            sp.dma_start(X4[:, 0:1024], d["s0"]).then_inc(in_s0, 16)
            sp.wait_ge(rw_done, 1)
            sp.dma_start(rc[:, 0:N_SC], d["sc"]).then_inc(in_sc, 16)
            last_page = d["cache_kv"].shape[1] - 1
            sp.wait_ge(in_const, 16 * 4)

            def page_at(n):
                return bass.ds(sp.value_load(pt_sb[0:1, n:n + 1], min_val=0, max_val=last_page), 1)

            def load_k(n):
                src = d["cache_kv"][0, page_at(n), :, 0, :, :].rearrange("n t h c -> (n t) (h c)")
                if n >= NKR:
                    sp.wait_ge(kt_ps, 2 * (n - NKR + 1))
                sp.dma_start(Kr[:, n % NKR, :], src).then_inc(in_k[n % NKR], 16)

            def load_v(n):
                src = d["cache_kv"][0, page_at(n), :, 1, :, :].rearrange("n t h c -> (n t) (h c)")
                if n >= NPG:
                    sp.wait_ge(spv_ps, n // NPG)
                sp.dma_start(Vr[:, n % NPG, :], src).then_inc(in_v[n % NPG], 16)

            for n in range(NKR):
                load_k(n)
            for n in range(DB * NPG):
                b, p = divmod(n, NPG)
                sp.dma_start(Call[4 * b:4 * b + 4, p * PAGE:(p + 1) * PAGE],
                             d["logf_t"][page_at(n), :, :].rearrange("n h t -> (n h) t")).then_inc(in_lf, 16)
            for n in range(NKR, NPG):
                load_k(n)
            for n in range(DB * NPG):
                if n + NPG < DB * NPG:
                    load_k(n + NPG)
                load_v(n)
            sp.wait_ge(spv_ps, DB)
            sp.wait_ge(stored, 16 * 12)
            for i, (t0, nr) in enumerate(TILES):
                sp.dma_start(x2[0:nr, i, :], xrows(i)).then_inc(in_resid, 16)
            for n in range(P_OUT + NW, len(pieces)):
                load_w(n)
            for i, (t0, nr) in enumerate(TILES):
                sp.wait_ge(y_ready, 6 + i)
                sp.dma_start(orows("y", i, 0, D), x2[0:nr, i, :]).then_inc(y_stored, 16)
            sp.wait_ge(y_stored, 16 * 5)
            sp.wait_ge(stored, 16 * (5 + 5 + 2))
            sp.wait_ge(k_out, 16 * 10)
            sp.wait_ge(shift_out, 16 * 2)

        @block.gpsimd
        def _(pool):
            pool.wait_ge(shift_ev, 1)
            pool.dma_start(o["shift_prompt"], shift_sb[0:1, :]).then_inc(shift_out, 16)
            pool.dma_start(o["shift_sample"], shift_sb[1:9, :]).then_inc(shift_out, 16)
            for g in (2, 3):
                pool.wait_ge(qk_normed, 5 * (g + 1))
                for i, (t0, nr) in enumerate(TILES):
                    c0 = (g - 2) * QC
                    pool.dma_start(orows("kv", i, c0, c0 + QC), ring[0:nr, g % 2, i, :]).then_inc(k_out, 16)
            pool.wait_ge(qkv_ev, 30)
            for i, (t0, nr) in enumerate(TILES):
                pool.dma_start(orows("kv", i, AW, 2 * AW), V[0:nr, i, :]).then_inc(stored, 16)
            pool.wait_ge(logf_ready, 1)
            for i, (t0, nr) in enumerate(TILES):
                pool.dma_start(orows("logf", i, 0, 4), logf[0:nr, 4 * i:4 * i + 4]).then_inc(stored, 16)
            pool.wait_ge(rw_done, 1)
            pool.dma_start(o["wkv_prompt"], X4[:, 3648:3776]).then_inc(stored, 16)
            pool.dma_start(o["wkv_sample"], X4[:, 0:1024]).then_inc(stored, 16)

        @block.tensor
        def _(pe):
            mm, turn = nc.tensor.matmul, nc.tensor.transpose

            pe.wait_ge(in_const, 16 * 4)
            for i, (t0, nr) in enumerate(TILES):
                pe.wait_ge(xs_ready, i + 1)
                if i >= 2:
                    pe.wait_ge(hT_ready, i - 1)
                base = (i % 2) * 1024
                for k in range(KT):
                    last = turn(PS[:, base + k * 128:base + k * 128 + nr], xs[0:nr, i, k * 128:(k + 1) * 128],
                                ident[0:nr, 0:nr])
                last.then_inc(xT_ps, 1)

            pe.wait_ge(hT_ready, 5)
            for m in range(8):
                w_wait(pe, m // 4)
                if m >= 4:
                    pe.wait_ge(p_ready, m - 3)
                out = pair(m % 4)
                for k in range(KT):
                    for a in range(2):
                        last = mm(out[:, a, :], wview(m // 4)[:, k, (m % 4) * 128:(m % 4 + 1) * 128],
                                  hT[:, k, a * 288:(a + 1) * 288], start=(k == 0), stop=(k == KT - 1))
                last.then_inc(p_ps, 1)

            def gemm(g):
                w_wait(pe, 2 + g)
                for t, (t0, nr) in enumerate(TILES):
                    n = g * 5 + t
                    if n >= 4:
                        pe.wait_ge(qkv_ev, n - 3)
                    for k in range(KT):
                        last = mm(PS[0:nr, (n % 4) * 512:(n % 4) * 512 + QW[g]], hT[:, k, t0:t0 + nr],
                                  wview(2 + g)[:, k, :], start=(k == 0), stop=(k == KT - 1))
                    last.then_inc(qkv_ps, 1)

            def turn_qk(g):
                for t, (t0, nr) in enumerate(TILES):
                    r = g * 5 + t
                    pe.wait_ge(qk_normed, r + 1)
                    if r >= 2:
                        pe.wait_ge(tr_ev, r - 1)
                    base = (6 + r % 2) * 512
                    for j in range(3):
                        last = turn(PS[:, base + j * 128:base + j * 128 + nr],
                                    ring[0:nr, g % 2, t, j * 128:(j + 1) * 128], ident[0:nr, 0:nr])
                    last.then_inc(tr_ps, 1)

            def head_sums(j0, slot_n):
                for a in range(2):
                    j = j0 + a
                    if j:
                        pe.wait_ge(hs_ev, j)
                    src = slot(slot_n)[:, a, :]
                    for hf in range(2):
                        last = mm(pair(2)[:, hf, :], ones_head, src[:, hf * 288:(hf + 1) * 288], start=True, stop=True)
                    last.then_inc(hs_ps, 1)

            pe.wait_ge(p_ready, 8)
            for m in range(8):
                last = turn(PS[0:9, 2048 + m * 128:2048 + (m + 1) * 128], pT[:, m, SEQ - 1:T:DT], ident)
            last.then_inc(shift_ps, 1)
            gemm(0)
            pe.wait_ge(lact, 2)
            pe.wait_ge(in_lora, 32)
            pe.wait_ge(shift_ev, 1)
            for j in range(6):
                if j:
                    pe.wait_ge(lora_ev, j)
                rows = (slice(0, 64), slice(64, 128), slice(0, 128))[j // 2]
                lhs = lora[rows, (0, 0, 256)[j // 2] + (j % 2) * 128:][:, 0:128]
                for hf in range(2):
                    last = mm(pair(2)[:, hf, :], lhs, xm[rows, (6, 6, 7)[j // 2], hf * 288:(hf + 1) * 288],
                              start=True, stop=True)
                last.then_inc(lora_ps, 1)
            gemm(1)
            turn_qk(0)
            pe.wait_ge(lora_ev, 6)
            pe.wait_ge(kksq_ready, 1)
            head_sums(0, 12)
            pe.wait_ge(bonus_in, 1)
            head_sums(2, 13)
            gemm(2)
            turn_qk(1)
            gemm(3)
            turn_qk(2)
            gemm(4)
            turn_qk(3)
            gemm(5)

            pe.wait_ge(ops_ready, 1)
            pe.wait_ge(qkv_ev, 30)
            pe.wait_ge(tr_ev, 20)
            pe.wait_ge(hs_ev, 4)
            pe.wait_ge(in_s0, 16)

            def begin(kind, a, *after):
                n = AT[kind, a]
                need = max([AT[x, a] + 1 for x in after] + ([n - 3] if n >= 4 else []), default=0)
                if need:
                    pe.wait_ge(c_ev, need)
                return (n % 4) * 1024

            def per_chunk(base, a, A, B, chunks=range(NCH), start=True, stop=True):
                for c in chunks:
                    for h in (slice(0, 64), slice(64, 128)):
                        last = mm(PS[h, base + c * CH:base + (c + 1) * CH], chunked(A)[h, a, c, :],
                                  B(h, a, c) if callable(B) else chunked(B)[h, a, c, :], start=start, stop=stop)
                return last

            def eye(h, a, c):
                return cst[h, K_ID:K_ID + 128][:, h]

            for kind, A, B in (("LT", 8, 1), ("L", 1, 8), ("ArbT", 8, 4), ("LkT", 3, 1), ("ArkT", 3, 4),
                               ("Vt", 6, eye), ("KQt", 1, eye), ("BEt", 9, eye), ("KEt", 5, eye)):
                for a in range(2):
                    base = begin(kind, a)
                    per_chunk(base, a, A, B).then_inc(c_ps, 1)
            for lev in range(5):
                for a in range(2):
                    base = begin(f"W{lev}", a, "L" if lev == 0 else f"dX{lev - 1}", "KEt")
                    pe.wait_ge(ltm_ready, 2 * lev + a + 1)
                    per_chunk(base, a, 3, 2).then_inc(c_ps, 1)
                if lev < 4:
                    for a in range(2):
                        base = begin(f"dX{lev}", a, f"W{lev}")
                        per_chunk(base, a, 8, 5).then_inc(c_ps, 1)
                for a in range(2):
                    base = begin(f"dXT{lev}", a, f"W{lev}")
                    per_chunk(base, a, 5, 8).then_inc(c_ps, 1)
            for kind, A, B, after in (("T1", 7, 14, ()), ("HT", 15, 8, ("dXT4",)), ("H", 8, 15, ()), ("G", 8, 9, ("T1",))):
                for a in range(2):
                    base = begin(kind, a, *after)
                    per_chunk(base, a, A, B).then_inc(c_ps, 1)
            for a in range(2):
                base = begin("MT", a, "H")
                per_chunk(base, a, 1, 17, range(8)).then_inc(c_ps, 1)
            for a in range(2):
                base = begin("N", a, "G")
                for c in range(8):
                    per_chunk(base, a, 18, 14, [c], stop=False)
                    last = per_chunk(base, a, 17, 19, [c], start=False)
                last.then_inc(c_ps, 1)
            pe.wait_ge(s1_ready, 1)
            for c in range(1, 8):
                n = AT[f"seq{c}", 0]
                pe.wait_ge(c_ev, n)
                for a in range(2):
                    for h in (slice(0, 64), slice(64, 128)):
                        last = mm(PS[h, (n % 4) * 1024 + a * 64:(n % 4) * 1024 + (a + 1) * 64],
                                  chunked(2)[h, a, c, :], chunked(5)[h, a, c, :], start=True, stop=True)
                last.then_inc(c_ps, 1)
            pe.wait_ge(masked_ready, 1)
            for a in range(2):
                base = begin("U", a)
                pe.wait_ge(c_ev, AT["seq7", 0] + 1)
                per_chunk(base, a, 0, 5, range(1, 8))
                for h in (slice(0, 64), slice(64, 128)):
                    for b in range(DB):
                        last = mm(PS[h, base + 8 * CH:base + 9 * CH], hexp[h, a, b, :], S0[h, a, b, :],
                                  start=(b == 0), stop=(b == DB - 1))
                last.then_inc(c_ps, 1)
            for a in range(2):
                base = begin("Y", a, "U")
                for c in range(NCH):
                    per_chunk(base, a, 9, 11, [c], stop=False)
                    if 1 <= c < 8:
                        per_chunk(base, a, 5, 4, [c], start=False, stop=False)
                    if c == 8:
                        for h in (slice(0, 64), slice(64, 128)):
                            for b in range(DB):
                                c0 = SEQ + b * DT
                                mm(PS[h, base + c0:base + c0 + DT], S0[h, a, b, :], slot(4)[h, a, c0:c0 + DT],
                                   start=False, stop=False, skip_group_check=True)
                    last = per_chunk(base, a, 14, 12, [c], start=False)
                last.then_inc(c_ps, 1)
            pe.wait_ge(masked_ready, 2)
            for a in range(2):
                base = begin("SS", a)
                for h in (slice(0, 64), slice(64, 128)):
                    mm(PS[h, base:base + 512], chunked(17)[h, a, 8, :], uexp[h, a, :, :], start=True, stop=False)
                    last = mm(PS[h, base:base + 512], chunked(18)[h, a, 8, :], hexp[h, a, :, :], start=False, stop=True)
                last.then_inc(c_ps, 1)
            for kind, src, after in (("GM", 6, "Y"), ("GV", 3, "GM")):
                for a in range(2):
                    begin(kind, a, after)
                    out = pair(AT[kind, a] % 4)
                    for hf in range(2):
                        last = mm(out[:, hf, :], ones_head, slot(src)[:, a, hf * 288:(hf + 1) * 288], start=True, stop=True)
                    last.then_inc(c_ps, 1)

            pe.wait_ge(c_ev, len(STEPS))
            pe.wait_ge(logf_ready, 1)
            for i in range(4):
                turn(PS[0:4, i * 128:(i + 1) * 128], logf[:, 4 * i:4 * i + 4], ident)
            pe.wait_ge(in_sc, 16)
            pe.wait_ge(lfx_ready, 1)
            mm(PS[0:32, 512:512 + NS], lfx, ident[0:NS, 0:NS], start=True, stop=True).then_inc(lt_ps, 1)
            pe.wait_ge(cT_ready, 1)
            for h in range(4):
                mm(PS[:, (2 + h) * 512:(3 + h) * 512], rc[0:4, S_HOT + h * 128:S_HOT + (h + 1) * 128], cT,
                   start=True, stop=True).then_inc(cb_ps, 1)
            pe.wait_ge(cb_ready, 4)
            pe.wait_ge(lfn_ready, 1)

            def scores(u):
                qt, h = UNITS[u]
                nk = (qt + 1) * 128
                if u >= 3:
                    pe.wait_ge(p_out, u - 2)
                rows = slice(64 * (h % 2), 64 * (h % 2) + 64)
                mm(PS[:, (u % 3) * 512:(u % 3) * 512 + nk], qT[rows, h // 2, qt * 128:(qt + 1) * 128],
                   kT[rows, h // 2, 0:nk], start=True, stop=True).then_inc(s_ps, 1)

            def turn_p(u):
                qt, h = UNITS[u]
                pe.wait_ge(p_out, u + 1)
                if u >= 2:
                    pe.wait_ge(pt_ev, u - 1)
                base = (3 + u % 2) * 512
                for j in range(qt + 1):
                    last = turn(PS[:, base + j * 128:base + (j + 1) * 128], Pp[:, u % NP_, j * 128:(j + 1) * 128], ident)
                last.then_inc(pt_ps, 1)

            def times_v(u):
                qt, h = UNITS[u]
                pe.wait_ge(pt_ev, u + 1)
                if u >= 2:
                    pe.wait_ge(pv_ev, u - 1)
                c0 = (5 + u % 2) * 512
                for j in range(qt + 1):
                    last = mm(PS[:, c0:c0 + 64], PTp[:, u % 2, j * 128:(j + 1) * 128], V[:, j, h * HD:(h + 1) * HD],
                              start=(j == 0), stop=(j == qt))
                last.then_inc(pv_ps, 1)

            def turn_y(qt):
                pe.wait_ge(pv_ev, 12 * (qt + 1))
                for n in range(2):
                    if 2 * qt + n:
                        pe.wait_ge(mt_ev, 2 * qt + n)
                    for j in range(3):
                        c0 = (3 * n + j) * 128
                        last = turn(PS[:, 7 * 512 + j * 128:7 * 512 + (j + 1) * 128], Ya[:, qt % 2, c0:c0 + 128], ident)
                    last.then_inc(mt_ps, 1)

            for i in range(NU + 5):
                if i < NU:
                    scores(i)
                if 0 <= i - 2 < NU:
                    turn_p(i - 2)
                if 0 <= i - 3 < NU:
                    times_v(i - 3)
                if i >= 16 and (i - 16) % 12 == 0:
                    turn_y((i - 16) // 12)

            def sampled_scores(b):
                if b >= 1:
                    pe.wait_ge(z_exp, 2 * b)
                pe.wait_ge(qbd_ready, b + 1)
                for g in range(NPG // 2):
                    for p in (2 * g, 2 * g + 1):
                        n = b * NPG + p
                        pe.wait_ge(in_k[n % NKR], 16 * (n // NKR + 1))
                        for q in range(2):
                            m = 2 * n + q
                            if m >= 3:
                                pe.wait_ge(kt_ev, m - 2)
                            base = (3 + m % 3) * 512
                            for c in range(3):
                                last = turn(PS[:, base + c * 128:base + (c + 1) * 128],
                                            Kr[:, n % NKR, (3 * q + c) * 128:(3 * q + c + 1) * 128], ident)
                            last.then_inc(kt_ps, 1)
                    pe.wait_ge(kt_ev, 2 * (b * NPG + 2 * g + 2))
                    n = b * NPG // 2 + g
                    for x in range(3):
                        for k in range(2):
                            last = mm(PS[32 * x:32 * x + 32, g * 256:(g + 1) * 256], qbd[:, b % 2, 2 * x + k, :],
                                      KTb[:, n % 2, 2 * x + k, :], start=(k == 0), stop=(k == 1 and x > 0))
                    if b == 0 and g == 0:
                        pe.wait_ge(call_ready, 1)
                    mm(PS[0:32, g * 256:(g + 1) * 256], rc[0:32, S_HB + 32 * b:S_HB + 32 * b + 32],
                       Call[:, g * 256:(g + 1) * 256], start=False, stop=True).then_inc(sg_ps, 1)
                for x in range(3):
                    for k in range(2):
                        mm(PS[32 * x:32 * x + 32, PAST:KEYS], qbd[:, b % 2, 2 * x + k, :],
                           kT[:, 2 * x + k, SEQ:T], start=(k == 0), stop=(k == 1 and x > 0))
                mm(PS[0:32, PAST:KEYS], rc[0:32, S_HB + 32 * b:S_HB + 32 * b + 32], Call[:, PAST:KEYS],
                   start=False, stop=True).then_inc(ss_ps, 1)

            def sampled_values(b):
                pe.wait_ge(pn_ready, b + 1)
                for jj in range(2):
                    n = 2 * b + jj
                    if n:
                        pe.wait_ge(spt_ev, n)
                    for j in range(5 * jj, min(5 * jj + 5, 9)):
                        nk = min(128, KEYS - j * 128)
                        base = 7 * 512 + (j % 5) * 96
                        last = turn(PS[0:nk, base:base + 96], Z[:, b % 2, j * 128:j * 128 + nk], ident[0:96, 0:96])
                    last.then_inc(spt_ps, 1)
                pe.wait_ge(spt_ev, 2 * b + 2)
                for p in range(NPG):
                    pe.wait_ge(in_v[p], 16 * (b + 1))
                if b >= 1:
                    pe.wait_ge(spv_ev, 2 * b)
                for c in range(6):
                    out = PS[:, 6 * 512 + 16 * c:6 * 512 + 16 * c + 16]
                    for j in range(NPG):
                        mm(out, Vr[:, j, c * 128:(c + 1) * 128], PTs[:, j, 16 * c:16 * c + 16],
                           start=(j == 0), stop=False)
                    last = mm(out, V[0:NS, 4, c * 128:(c + 1) * 128], PTs[0:NS, 8, 16 * c:16 * c + 16],
                              start=False, stop=True)
                last.then_inc(spv_ps, 1)

            pe.wait_ge(mt_ev, 8)
            for b in range(DB + 1):
                if b < DB:
                    sampled_scores(b)
                if b >= 1:
                    sampled_values(b - 1)

            pe.wait_ge(spv_ev, 2 * DB)
            pe.wait_ge(rw_done, 1)
            for g in range(2):
                w_wait(pe, P_OUT + g)
                for t, (t0, nr) in enumerate(TILES):
                    n = g * 5 + t
                    if n >= 8:
                        pe.wait_ge(o_ev, n - 7)
                    for k in range(KT):
                        last = mm(PS[0:nr, (n % 8) * 512:(n % 8 + 1) * 512], mixT[:, k, t0:t0 + nr],
                                  wview(P_OUT + g)[:, k, :], start=(k == 0), stop=(k == KT - 1))
                    last.then_inc(o_ps, 1)
            pe.wait_ge(o_ev, 10)
            for i, (t0, nr) in enumerate(TILES):
                pe.wait_ge(x2s_ready, i + 1)
                if i >= 2:
                    pe.wait_ge(h2_ready, i - 1)
                base = (i % 2) * 1024
                for k in range(KT):
                    last = turn(PS[:, base + k * 128:base + k * 128 + nr], xs[0:nr, i, k * 128:(k + 1) * 128],
                                ident[0:nr, 0:nr])
                last.then_inc(h2_ps, 1)
            pe.wait_ge(h2_ready, 5)
            for f in range(32):
                w_wait(pe, P_UP + f // 4)
                if f >= 4:
                    pe.wait_ge(u_ev, f - 3)
                out = pair(f % 4)
                for k in range(KT):
                    for a in range(2):
                        last = mm(out[:, a, :], wview(P_UP + f // 4)[:, k, (f % 4) * 128:(f % 4 + 1) * 128],
                                  h2T[:, k, a * 288:(a + 1) * 288], start=(k == 0), stop=(k == KT - 1))
                last.then_inc(u_ps, 1)
            pe.wait_ge(u_sq, 32)
            for n in range(2):
                def down(g, k, t):
                    t0, nr = TILES[t]
                    bank = (5 * n + t) % 8
                    return mm(PS[0:nr, bank * 512:(bank + 1) * 512], uT[:, 8 * g + k, t0:t0 + nr],
                              wview(P_DN + 4 * n + g)[:, k, :], start=(g == 0 and k == 0), stop=(g == 3 and k == 7))
                for g in range(4):
                    w_wait(pe, P_DN + 4 * n + g)
                    for t in range(5):
                        if n == 1 and g == 0 and 5 + t >= 8:
                            pe.wait_ge(y_ready, 5 + t - 7)
                        for k in range(8):
                            last = down(g, k, t)
                        if g == 3:
                            last.then_inc(y_ps, 1)
                        elif t == 4:
                            last.then_inc(dn_used, 1)

        @block.scalar
        def _(act):
            steps = [0]

            def link(ins):
                steps[0] += 1
                ins.then_inc(a_step, 1)
                act.wait_ge(a_step, steps[0])

            f = nc.scalar.activation

            act.wait_ge(init, 1)
            for i, (t0, nr) in enumerate(TILES):
                act.wait_ge(in_x[i], 16)
                f(xs[0:nr, i, :], xin[0:nr, i, :], ACT.Square, accum_out=ssq[0:nr, i:i + 1]).then_inc(squares, 1)
            act.wait_ge(squares, 5)
            f(rstd, ssq, ACT.Sqrt, scale=1.0 / D, bias=eps).then_inc(std_ready, 1)

            for m in range(8):
                act.wait_ge(p_ps, m + 1)
                f(halves(pT[:, m, :]), pair(m % 4), ACT.Copy).then_inc(p_ready, 1)

            def take(g):
                for t, (t0, nr) in enumerate(TILES):
                    r = g * 5 + t
                    act.wait_ge(qkv_ps, r + 1)
                    src = PS[0:nr, (r % 4) * 512:(r % 4) * 512 + QC]
                    if g >= 4:
                        if g == 5:
                            f(logf[0:nr, 4 * t:4 * t + 4], PS[0:nr, (r % 4) * 512 + QC:(r % 4) * 512 + QC + 4], ACT.Copy)
                        f(V[0:nr, t, (g - 4) * QC:(g - 3) * QC], src, ACT.Copy).then_inc(qkv_ev, 1)
                        continue
                    if g >= 2 and t == 0:
                        act.wait_ge(tr_ps, 5 * (g - 1))
                    f(ring[0:nr, g % 2, t, :], src, ACT.Copy).then_inc(qkv_ev, 1)
                    if r >= 3:
                        act.wait_ge(sq_used, r - 2)
                    act.wait_ge(qkv_ev, r + 1)
                    nh = (6, 2)[g % 2]
                    f(sqtmp[0:nr, r % 3, 0:nh * HD], ring[0:nr, g % 2, t, 0:nh * HD], ACT.Square).then_inc(sq_ready, 1)
                if g < 4:
                    act.wait_ge(sq_used, 5 * (g + 1))
                    f(qrs, qss, ACT.Sqrt, scale=1.0 / HD, bias=eps).then_inc(qstd_ready, 1)

            take(0)
            act.wait_ge(xm_ready, 1)
            f(xm[0:64, 6, :], xm[0:64, 6, :], ACT.Tanh).then_inc(lact, 1)
            f(xm[:, 7, :], xm[:, 7, :], ACT.Sigmoid).then_inc(lact, 1)
            for j in range(6):
                act.wait_ge(lora_ps, j + 1)
                dst = halves(slot((8, 9, 10)[j // 2])[:, j % 2, :])
                if j < 4:
                    c = (C_W0, C_A0)[j // 2] + j % 2
                    f(dst, pair(2), ACT.Sigmoid, bias=prm[:, c:c + 1]).then_inc(lora_ev, 1)
                else:
                    f(dst, pair(2), ACT.Copy).then_inc(lora_ev, 1)
            take(1)
            act.wait_ge(hs_ev, 2)
            f(slot(12), slot(12), ACT.Sqrt).then_inc(kkstd_ready, 1)
            take(2)
            act.wait_ge(exp_in, 1)
            for dst, src, sign in ((1, 1, 1.0), (2, 0, 1.0), (3, 0, -1.0), (7, 7, 1.0)):
                f(slot(dst), slot(src), ACT.Exp, scale=sign).then_inc(exp_out, 1)
            take(3)
            take(4)
            take(5)
            act.wait_ge(logf_in, 1)
            nc.scalar.preload_act_table_set("natural_log_exp_and_others")
            link(f(ftmp, ftmp, ACT.Exp))
            f(ftmp, ftmp, ACT.Ln, bias=1.0).then_inc(logf_a, 1)

            act.wait_ge(c_ev, len(STEPS))
            f(slot(3), slot(3), ACT.Sqrt, bias=gneps).then_inc(gnstd_ready, 1)

            nc.scalar.preload_act_table_set("natural_log_exp_and_others")
            act.wait_ge(rw_done, 1)
            for h in range(4):
                act.wait_ge(cb_ps, h + 1)
                f(cb[:, h, :], PS[:, (2 + h) * 512:(3 + h) * 512], ACT.Copy).then_inc(cb_ready, 1)

            n_in, n_sb = 0, 0
            for i in range(NU + 3):
                if i < NU and is_sb(i):
                    nk = (UNITS[i][0] + 1) * 128
                    act.wait_ge(a_in, i + 1)
                    link(f(T1p[:, i % 2, 0:nk], T1p[:, i % 2, 0:nk], ACT.Exp))
                    f(T1p[:, i % 2, 0:nk], T1p[:, i % 2, 0:nk], ACT.Ln, bias=1.0).then_inc(a_mid, 1)
                if is_sb(i - 1):
                    u = i - 1
                    nk = (UNITS[u][0] + 1) * 128
                    n_sb += 1
                    act.wait_ge(sb_in, n_sb)
                    if u >= NP_:
                        act.wait_ge(pt_ps, u - NP_ + 1)
                    f(Pp[:, u % NP_, 0:nk], T1p[:, u % 2, 0:nk], ACT.Exp, bias=nmax[:, u % 8:u % 8 + 1]).then_inc(p_out, 1)
                if i < NU and not is_sb(i):
                    nk = (UNITS[i][0] + 1) * 128
                    act.wait_ge(a_in, i + 1)
                    if i >= NP_:
                        act.wait_ge(pt_ps, i - NP_ + 1)
                    f(Pp[:, i % NP_, 0:nk], PS[:, (i % 3) * 512:(i % 3) * 512 + nk], ACT.Exp,
                      bias=nmax[:, i % 8:i % 8 + 1], accum_out=rsum[:, i % 8:i % 8 + 1]).then_inc(p_out, 1)
                u = i - 2
                if 0 <= u < NU:
                    nk = (UNITS[u][0] + 1) * 128
                    act.wait_ge(pt_ps, u + 1)
                    if u >= 2:
                        act.wait_ge(pv_ps, u - 1)
                    f(PTp[:, u % 2, 0:nk], PS[:, (3 + u % 2) * 512:(3 + u % 2) * 512 + nk], ACT.Copy).then_inc(pt_ev, 1)
                if i >= 16 and (i - 16) % 12 == 0:
                    take_y(nc, act, (i - 16) // 12, mt_ps, mt_ev, mixT, PS)
            take_y(nc, act, 3, mt_ps, mt_ev, mixT, PS)

            def take_pages(b):
                for p in range(NPG):
                    n = b * NPG + p
                    g = n // 2
                    if g >= 2 and p % 2 == 0:
                        act.wait_ge(sg_ps, g - 1)
                    for q in range(2):
                        m = 2 * n + q
                        act.wait_ge(kt_ps, m + 1)
                        base = (3 + m % 3) * 512
                        f(KTb[:, g % 2, 3 * q:3 * q + 3, (p % 2) * 128:(p % 2 + 1) * 128],
                          PS[:, base:base + 384].rearrange("p (c k) -> p c k", c=3), ACT.Copy).then_inc(kt_ev, 1)

            def softmax_part(b):
                act.wait_ge(z_abs, b + 1)
                link(f(T1[64:96, :], T1[64:96, :], ACT.Exp))
                f(T1[64:96, :], T1[64:96, :], ACT.Ln, bias=1.0).then_inc(z_ln, 1)
                act.wait_ge(z_max, b + 1)
                if b >= 2:
                    act.wait_ge(spt_ps, 2 * (b - 1))
                f(Z[0:64, b % 2, :], PS[0:64, 0:KEYS], ACT.Exp, bias=nmax[0:64, 0:1],
                  accum_out=rsum[0:64, 0:1]).then_inc(z_exp, 1)
                act.wait_ge(z_sb, b + 1)
                f(Z[64:96, b % 2, :], T1[64:96, :], ACT.Exp, bias=nmax[64:96, 0:1]).then_inc(z_exp, 1)

            def take_values(b):
                act.wait_ge(spv_ps, b + 1)
                src = PS[:, 6 * 512:6 * 512 + 96].rearrange("p (c q) -> p c q", c=6)
                c0 = SEQ + b * DT
                for hf in range(2):
                    rows = slice(64 * hf, 64 * hf + 64)
                    f(mixT[rows, 2:8, c0:c0 + DT], src[rows, :, 8 * hf:8 * hf + 8], ACT.Copy).then_inc(spv_ev, 1)

            for b in range(DB + 1):
                if b < DB:
                    take_pages(b)
                    softmax_part(b)
                if b >= 1:
                    take_values(b - 1)

            for i, (t0, nr) in enumerate(TILES):
                act.wait_ge(o_ev, 6 + i)
                f(xs[0:nr, i, :], x2[0:nr, i, :], ACT.Square, accum_out=ssq[0:nr, i:i + 1]).then_inc(x2_ssq, 1)
                act.wait_ge(x2_ssq, i + 1)
                f(rstd[:, i:i + 1], ssq[:, i:i + 1], ACT.Sqrt, scale=1.0 / D, bias=eps).then_inc(x2_std, 1)
            for n in range(32):
                act.wait_ge(u_ps, n + 1)
                f(halves(uT[:, n, :]), pair(n % 4), ACT.Relu).then_inc(u_ev, 1)

        @block.vector
        def _(dve):
            steps = [0]

            def link(ins):
                steps[0] += 1
                ins.then_inc(v_step, 1)
                dve.wait_ge(v_step, steps[0])

            tt, ts, stt = nc.vector.tensor_tensor, nc.vector.tensor_scalar, nc.vector.scalar_tensor_tensor
            copy, red, recip = nc.vector.tensor_copy, nc.vector.tensor_reduce, nc.vector.reciprocal
            MUL, ADD, SUB, MAX, MIN = ALU.mult, ALU.add, ALU.subtract, ALU.max, ALU.min

            def col(c):
                return prm[:, c:c + 1]

            link(nc.vector.memset(small[:, 0:128], 0.0))
            link(nc.vector.memset(small[:, 16:76], 1.0))
            link(nc.vector.memset(eps, RMS_EPS))
            link(nc.vector.memset(onec, 1.0))
            nc.vector.memset(gneps, GN_EPS).then_inc(init, 1)
            dve.wait_ge(in_const, 16 * 4)
            dve.wait_ge(std_ready, 1)
            link(recip(rstd, rstd))
            for i, (t0, nr) in enumerate(TILES):
                ts(xs[0:nr, i, :], xin[0:nr, i, :], rstd[0:nr, i:i + 1], None, MUL).then_inc(xs_ready, 1)

            def take_turned(i, dst, g0, done):
                t0, nr = TILES[i]
                base = (i % 2) * 1024
                tt(dst[:, :, t0:t0 + nr], PS[:, base:base + 1024].rearrange("p (k t) -> p k t", k=8)[:, :, 0:nr],
                   prm[:, g0:g0 + 8].unsqueeze(2).to_broadcast([128, 8, nr]), MUL).then_inc(done, 1)

            for i in range(5):
                dve.wait_ge(xT_ps, i + 1)
                take_turned(i, hT, C_AN, hT_ready)
            ts(omka, prm[:, C_KA:C_KA + 2], -1.0, 1.0, MUL, ADD).then_inc(v_step, 1)
            steps[0] += 1
            link(ts(gq, prm[:, C_QN:C_QN + 6], HD ** -0.5, None, MUL))

            dve.wait_ge(p_ready, 8)
            tt(xm[:, :, 1:SEQ], pT[:, :, 0:SEQ - 1], pT[:, :, 1:SEQ], SUB).then_inc(v_step, 1)
            ts(xm[:, :, 0:1], pT[:, :, 0:1], -1.0, None, MUL).then_inc(v_step, 1)
            steps[0] += 2
            for m in range(8):
                xs4 = xm[:, m, SEQ:].rearrange("p (b t) -> p b t", t=DT)
                ps4 = pT[:, m, SEQ:].rearrange("p (b t) -> p b t", t=DT)
                tt(xs4[:, :, 1:DT], ps4[:, :, 0:DT - 1], ps4[:, :, 1:DT], SUB).then_inc(v_step, 1)
                tt(xs4[:, :, 0:1], shift0[:, m, :].unsqueeze(2), ps4[:, :, 0:1], SUB).then_inc(v_step, 1)
                steps[0] += 2
            dve.wait_ge(v_step, steps[0])
            for m in range(8):
                ins = stt(xm[:, m, :], xm[:, m, :], col(C_MU + m), pT[:, m, :], MUL, ADD)
                if m < 7:
                    ins.then_inc(v_step, 1)
                    steps[0] += 1
            ins.then_inc(xm_ready, 1)
            dve.wait_ge(xm_ready, 1)
            dve.wait_ge(v_step, steps[0])
            dve.wait_ge(shift_ps, 1)
            copy(shift_sb, PS[0:9, 2048:3072]).then_inc(shift_ev, 1)
            link(nc.vector.memset(reset, 1.0))
            link(nc.vector.memset(reset[:, 0:SEQ:CH], 0.0))
            link(nc.vector.memset(reset[:, SEQ:T:DT], 0.0))

            def norm_sums(g):
                nh = (6, 2)[g % 2]
                if g:
                    dve.wait_ge(qstd_ready, g)
                for t, (t0, nr) in enumerate(TILES):
                    r = g * 5 + t
                    dve.wait_ge(sq_ready, r + 1)
                    red(qss[0:nr, t, 0:nh], sqtmp[0:nr, r % 3, 0:nh * HD].rearrange("p (h c) -> p h c", c=HD),
                        AX.X, ADD).then_inc(sq_used, 1)

            def norm_scale(g):
                nh = (6, 2)[g % 2]
                dve.wait_ge(qstd_ready, g + 1)
                link(recip(qrs, qrs))
                for t, (t0, nr) in enumerate(TILES):
                    x = ring[0:nr, g % 2, t, 0:nh * HD]
                    x3 = x.rearrange("p (h c) -> p h c", c=HD)
                    ins = tt(x3, x3, qrs[0:nr, t, 0:nh].unsqueeze(2).to_broadcast([nr, nh, HD]), MUL)
                    if g >= 2:
                        link(ins)
                        if g == 2 and t == 0:
                            dve.wait_ge(in_kn, 16)
                        ins = tt(x, x, knorm[0:nr, (g - 2) * QC:(g - 2) * QC + nh * HD], MUL)
                    ins.then_inc(qk_normed, 1)

            def take_qk(g):
                for t, (t0, nr) in enumerate(TILES):
                    r = g * 5 + t
                    dve.wait_ge(tr_ps, r + 1)
                    src = PS[:, (6 + r % 2) * 512:(6 + r % 2) * 512 + QC].rearrange("p (j t) -> p j t", j=3)[:, :, 0:nr]
                    c = 3 * (g % 2)
                    if g < 2:
                        ins = tt(qT[:, c:c + 3, t0:t0 + nr], src,
                                 gq[:, c:c + 3].unsqueeze(2).to_broadcast([128, 3, nr]), MUL)
                    else:
                        ins = copy(kT[:, c:c + 3, t0:t0 + nr], src)
                    ins.then_inc(tr_ev, 1)

            norm_sums(0)
            norm_scale(0)

            dve.wait_ge(lora_ev, 6)
            link(ts(slot(8), slot(8), DECAY, None, MUL))
            for a in range(2):
                link(nc.vector.tensor_tensor_scan(slot(0)[:, a, :], reset, slot(8)[:, a, :], 0.0, MUL, ADD))
            for a in range(2):
                link(ts(slot(11)[:, a, :], slot(5)[:, a, :], col(C_KK + a), None, MUL))
            tt(slot(12), slot(11), slot(11), MUL).then_inc(kksq_ready, 1)
            dve.wait_ge(shift_out, 32)
            for a in range(2):
                link(ts(slot(13)[:, a, :], slot(9)[:, a, :], col(C_KA + a), omka[:, a:a + 1], MUL, ADD))
            link(tt(slot(5), slot(5), slot(13), MUL))
            link(tt(slot(13), slot(4), slot(5), MUL))
            for a in range(2):
                ins = ts(slot(13)[:, a, :], slot(13)[:, a, :], col(C_RK + a), None, MUL)
                if a == 0:
                    link(ins)
            ins.then_inc(bonus_in, 1)
            norm_sums(1)
            norm_scale(1)
            take_qk(0)
            for a in range(2):
                dve.wait_ge(hs_ps, a + 1)
                if a == 0:
                    dve.wait_ge(kksq_ready, 1)
                ts(halves(slot(12)[:, a, :]), pair(2), 1e-24, None, MAX).then_inc(hs_ev, 1)
            for a in range(2):
                dve.wait_ge(hs_ps, 3 + a)
                tt(halves(slot(13)[:, a, :]), pair(2), halves(slot(6)[:, a, :]), MUL).then_inc(hs_ev, 1)
            link(tt(slot(1), slot(0), slot(8), SUB))
            for a in range(2):
                for s, n, w in ((slot(0)[:, a, 0:SEQ], 8, CH), (slot(0)[:, a, SEQ:T], 8, DT)):
                    lo = 0 if w == CH else SEQ
                    x = s.rearrange("p (c s) -> p c s", s=w)
                    y = slot(7)[:, a, lo:lo + n * w].rearrange("p (c s) -> p c s", s=w)
                    ins = tt(y, x[:, :, w - 1:w].to_broadcast([128, n, w]), x, SUB)
                    if a == 0 or w == CH:
                        link(ins)
            ins.then_inc(exp_in, 1)
            dve.wait_ge(kkstd_ready, 1)
            link(recip(slot(12), slot(12)))
            link(tt(slot(11), slot(11), slot(12), MUL))
            norm_sums(2)
            norm_scale(2)
            take_qk(1)
            dve.wait_ge(exp_out, 4)
            link(copy(pc[:, :, 0:8], slot(2)[:, :, CH - 1:SEQ:CH]))
            link(copy(pc[:, :, 8:16], slot(2)[:, :, SEQ + DT - 1:T:DT]))
            link(tt(slot(1), slot(1), slot(11), MUL))
            link(tt(slot(4), slot(4), slot(2), MUL))
            link(tt(slot(9), slot(9), slot(11), MUL))
            link(tt(slot(8), slot(9), slot(3), MUL))
            link(tt(slot(3), slot(5), slot(3), MUL))
            link(tt(slot(9), slot(9), slot(7), MUL))
            tt(slot(5), slot(5), slot(7), MUL).then_inc(ops_ready, 1)
            norm_sums(3)
            norm_scale(3)
            take_qk(2)
            take_qk(3)
            dve.wait_ge(qkv_ev, 30)
            lf3 = logf.rearrange("p (t h) -> p t h", h=4)
            link(tt(lf3, lf3, prm[:, C_BF:C_BF + 4].unsqueeze(1).to_broadcast([128, 5, 4]), ADD))
            ts(ftmp, logf, -1.0, SP_MAX, MUL, MIN).then_inc(logf_in, 1)
            dve.wait_ge(logf_a, 1)
            stt(logf, ftmp, -1.0, logf, MUL, MIN).then_inc(logf_ready, 1)
            dve.wait_ge(logf_ready, 1)
            copy(lfx.rearrange("p (b h) -> p b h", b=DB),
                 logf[0:NS, 16:20].unsqueeze(1).to_broadcast([NS, DB, 4])).then_inc(lfx_ready, 1)

            dve.wait_ge(in_rc, 16)

            def take(kind, a):
                n = AT[kind, a]
                dve.wait_ge(c_ps, n + 1)
                return PS[:, (n % 4) * 1024:(n % 4) * 1024 + T]

            def r3(ap):
                return ap.rearrange("p (c s) -> p c s", s=CH)

            def mask64(c0, n=NCH):
                return rc[:, c0:c0 + 64].unsqueeze(1).to_broadcast([128, n, 64])

            id64 = cst[:, K_ID64:K_ID64 + 64].unsqueeze(1).to_broadcast([128, NCH, 64])

            for kind, dst, m in (("LT", 0, R_SU), ("L", 2, None), ("ArbT", 11, R_IU), ("LkT", 7, R_SU), ("ArkT", 12, R_IU)):
                for a in range(2):
                    src = take(kind, a)
                    if kind == "L":
                        link(tt(chunked(dst)[:, a], r3(src), mask64(R_L1), MUL))
                        tt(chunked(dst)[:, a], id64, chunked(dst)[:, a], SUB).then_inc(c_ev, 1)
                    else:
                        tt(slot(dst)[:, a, :], src, rc[:, m:m + T], MUL).then_inc(c_ev, 1)
            for kind, dst in (("Vt", 14), ("KQt", 15), ("BEt", 17), ("KEt", 18)):
                for a in range(2):
                    copy(slot(dst)[:, a, :], take(kind, a)).then_inc(c_ev, 1)
            dve.wait_ge(c_ev, AT["KEt", 1] + 1)
            for a in range(2):
                link(tt(chunked(8)[:, a], chunked(0)[:, a], mask64(R_L1T), MUL))
                link(tt(chunked(8)[:, a], id64, chunked(8)[:, a], SUB))
            for lev in range(5):
                for a in range(2):
                    if lev:
                        dve.wait_ge(c_ps, AT[f"W{lev - 1}", a] + 1)
                    tt(chunked(3)[:, a], chunked(0)[:, a], mask64(R_LEV + 64 * lev), MUL).then_inc(ltm_ready, 1)
                for a in range(2):
                    copy(slot(5)[:, a, :], take(f"W{lev}", a)).then_inc(c_ev, 1)
                for k, x in ((("dX", 2), ("dXT", 8)) if lev < 4 else (("dXT", 8),)):
                    for a in range(2):
                        src = take(f"{k}{lev}", a)
                        if x == 8 and lev < 4 or x == 2:
                            dve.wait_ge(c_ps, AT[f"dXT{lev}", a] + 1 if x == 8 else AT[f"dX{lev}", a] + 1)
                        tt(slot(x)[:, a, :], slot(x)[:, a, :], src, SUB).then_inc(c_ev, 1)
            dve.wait_ge(c_ev, AT["dXT4", 1] + 1)
            for a in range(2):
                copy(slot(9)[:, a, :], take("T1", a)).then_inc(c_ev, 1)
            for kind, dst in (("HT", 0), ("H", 1), ("G", 19)):
                for a in range(2):
                    ts(slot(dst)[:, a, :], take(kind, a), -1.0, None, MUL).then_inc(c_ev, 1)
            dve.wait_ge(c_ev, AT["G", 1] + 1)
            for a in range(2):
                link(tt(chunked(2)[:, a, 0:8], cst[:, K_ID64:K_ID64 + 64].unsqueeze(1).to_broadcast([128, 8, 64]),
                        pc[:, a, 0:8].unsqueeze(2).to_broadcast([128, 8, 64]), MUL))
                src = take("MT", a)
                tt(chunked(2)[:, a, 0:8], chunked(2)[:, a, 0:8], r3(src)[:, 0:8], ADD).then_inc(c_ev, 1)
            for a in range(2):
                copy(slot(3)[:, a, 0:SEQ], take("N", a)[:, 0:SEQ]).then_inc(c_ev, 1)
            dve.wait_ge(c_ev, AT["N", 1] + 1)
            dve.wait_ge(in_s0, 16)
            for a in range(2):
                ins = tt(hexp[:, a], chunked(0)[:, a, 8:9, :].to_broadcast([128, DB, 64]),
                         rc[:, R_BM:R_BM + 512].rearrange("p (b t) -> p b t", b=DB), MUL)
                if a == 0:
                    link(ins)
            ins.then_inc(masked_ready, 1)
            copy(chunked(5)[:, :, 1, :], chunked(3)[:, :, 0, :]).then_inc(s1_ready, 1)
            for c in range(1, 8):
                n = AT[f"seq{c}", 0]
                dve.wait_ge(c_ps, n + 1)
                src = PS[:, (n % 4) * 1024:(n % 4) * 1024 + 128].rearrange("p (a i) -> p a i", a=2)
                dst = chunked(5)[:, :, c + 1, :] if c < 7 else sfin
                tt(dst, src, chunked(3)[:, :, c, :], ADD).then_inc(c_ev, 1)
            for a in range(2):
                src = take("U", a)
                link(copy(slot(9)[:, a, 0:CH], slot(19)[:, a, 0:CH]))
                tt(slot(9)[:, a, CH:T], src[:, CH:T], slot(19)[:, a, CH:T], ADD).then_inc(c_ev, 1)
            for a in range(2):
                copy(slot(6)[:, a, :], take("Y", a)).then_inc(c_ev, 1)
            for a in range(2):
                bm = prm[:, C_BM:C_BM + DB].unsqueeze(2).to_broadcast([128, DB, 64])
                link(tt(uexp[:, a], chunked(9)[:, a, 8:9, :].to_broadcast([128, DB, 64]), bm, MUL))
                ins = tt(hexp[:, a], chunked(14)[:, a, 8:9, :].to_broadcast([128, DB, 64]), bm, MUL)
                if a == 0:
                    link(ins)
            ins.then_inc(masked_ready, 1)
            for a in range(2):
                link(tt(S0[:, a], S0[:, a], pc[:, a, 8:16].unsqueeze(2).to_broadcast([128, DB, 64]), MUL))
                src = take("SS", a)
                tt(S0[:, a], S0[:, a], src[:, 0:512].rearrange("p (b i) -> p b i", b=DB), ADD).then_inc(c_ev, 1)
            for a in range(2):
                dve.wait_ge(c_ps, AT["GM", a] + 1)
                y = halves(slot(6)[:, a, :])
                link(stt(y, pair(AT["GM", a] % 4), -1.0 / HD, y, MUL, ADD))
                tt(slot(3)[:, a, :], slot(6)[:, a, :], slot(6)[:, a, :], MUL).then_inc(c_ev, 1)
            for a in range(2):
                dve.wait_ge(c_ps, AT["GV", a] + 1)
                ts(halves(slot(3)[:, a, :]), pair(AT["GV", a] % 4), 1.0 / HD, None, MUL).then_inc(c_ev, 1)
            dve.wait_ge(gnstd_ready, 1)
            link(recip(slot(3), slot(3)))
            link(tt(slot(6), slot(6), slot(3), MUL))
            for a in range(2):
                link(ts(slot(6)[:, a, :], slot(6)[:, a, :], col(C_GW + a), col(C_GB + a), MUL, ADD))
            link(tt(slot(6), slot(6), slot(13), ADD))
            tt(mixT[:, 0:2, :], slot(6), slot(10), MUL).then_inc(rw_done, 1)

            dve.wait_ge(lt_ps, 1)
            link(copy(cT, PS[0:4, 0:SEQ]))
            nc.vector.tensor_tensor_scan(cT, onec[0:4].to_broadcast([4, SEQ]), cT, 0.0, MUL, ADD).then_inc(cT_ready, 1)
            dve.wait_ge(in_sc, 16)
            dve.wait_ge(cT_ready, 1)
            tt(Call[:, PAST:KEYS], PS[0:32, 512:512 + NS], rc[0:32, S_LM:S_LM + NS], MUL).then_inc(lfn_ready, 1)
            link(nc.vector.memset(T2p[:, 0:1], 0.0))
            dve.wait_ge(cb_ready, 4)

            n_mid = [0]

            def front(u):
                qt, h = UNITS[u]
                nk = (qt + 1) * 128
                z = PS[:, (u % 3) * 512:(u % 3) * 512 + nk]
                dve.wait_ge(s_ps, u + 1)
                if h < 4:
                    link(tt(z, z, cb[:, h, 0:nk], ADD))
                m = K_CAU if h < 8 else K_STR
                link(tt(z[:, nk - 128:nk], z[:, nk - 128:nk], cst[:, m:m + 128], ADD))
                if h < 8:
                    red(nmax[:, u % 8:u % 8 + 1], z, AX.X, MAX, negate=True).then_inc(a_in, 1)
                else:
                    if u >= 2:
                        dve.wait_ge(p_out, u - 1)
                    ts(T1p[:, u % 2, 0:nk], z, SP_MAX, None, MIN).then_inc(a_in, 1)

            def mid(u):
                qt, h = UNITS[u]
                nk = (qt + 1) * 128
                z = PS[:, (u % 3) * 512:(u % 3) * 512 + nk]
                t1 = T1p[:, u % 2, 0:nk]
                n_mid[0] += 1
                dve.wait_ge(a_mid, n_mid[0])
                link(tt(t1, z, t1, MAX))
                link(nc.vector.tensor_tensor_scan(T2p[:, 1:nk + 1], onec.to_broadcast([128, nk]), t1, 0.0, MUL, ADD))
                link(tt(t1, z, T2p[:, 0:nk], ADD))
                ts(nmax[:, u % 8:u % 8 + 1], T2p[:, nk:nk + 1], -1.0, None, MUL).then_inc(sb_in, 1)

            def take_out(u):
                qt, h = UNITS[u]
                dve.wait_ge(pv_ps, u + 1)
                if h == 0 and qt >= 2:
                    dve.wait_ge(mt_ps, 2 * (qt - 1))
                src = PS[:, (5 + u % 2) * 512:(5 + u % 2) * 512 + 64]
                dst = Ya[:, qt % 2, h * HD:(h + 1) * HD]
                if h < 8:
                    r = rinv[:, u % 8:u % 8 + 1]
                    link(recip(r, rsum[:, u % 8:u % 8 + 1]))
                    ts(dst, src, r, None, MUL).then_inc(pv_ev, 1)
                else:
                    copy(dst, src).then_inc(pv_ev, 1)

            for i in range(NU + 4):
                if i < NU:
                    front(i)
                if is_sb(i - 1):
                    mid(i - 1)
                if 0 <= i - 4 < NU:
                    take_out(i - 4)

            dve.wait_ge(mt_ps, 8)
            link(nc.vector.memset(qbd[:, :, :, :], 0.0))
            link(nc.vector.memset(T2[:, 0:1], 0.0))
            dve.wait_ge(in_lf, 16 * DB * NPG)
            dve.wait_ge(lfn_ready, 1)
            nc.vector.tensor_tensor_scan(Call, onec[0:32].to_broadcast([32, KEYS]), Call, 0.0, MUL, ADD).then_inc(call_ready, 1)

            def spread_q(b):
                if b >= 2:
                    dve.wait_ge(ss_ps, b - 1)
                c0 = SEQ + b * DT
                for k in range(2):
                    for hf in range(2):
                        rows = slice(64 * hf, 64 * hf + 64)
                        q0 = 16 * k + 8 * hf
                        ins = copy(qbd[rows, b % 2, k:6:2, q0:q0 + 8], qT[rows, k:6:2, c0:c0 + DT])
                        if (k, hf) != (1, 1):
                            link(ins)
                ins.then_inc(qbd_ready, 1)

            def sampled_softmax(b):
                dve.wait_ge(ss_ps, b + 1)
                new = PS[0:96, PAST:KEYS]
                link(tt(new, new, rc[0:96, S_MASK + 64 * b:S_MASK + 64 * b + 64], ADD))
                if b:
                    dve.wait_ge(z_exp, 2 * b)
                ts(T1[64:96, :], PS[64:96, 0:KEYS], SP_MAX, None, MIN).then_inc(z_abs, 1)
                m = slice(32, 64)
                old = PS[m, 0:PAST].rearrange("p (n k) -> p n k", n=NBLK)
                link(red(gate[m], old, AX.X, ADD))
                link(red(gmin[m, 0:1], gate[m], AX.X, MIN))
                link(ts(gsel[m], gate[m], gmin[m, 0:1], None, ALU.is_equal))
                link(tt(gsel[m], gsel[m], rc[m, S_IOTA:S_IOTA + NBLK], MUL))
                link(red(gmin[m, 1:2], gsel[m], AX.X, MAX))
                link(ts(gsel[m], gsel[m], gmin[m, 1:2], NEG, ALU.is_equal, MUL))
                link(tt(old, old, gsel[m].unsqueeze(2).to_broadcast([32, NBLK, BLK]), ADD))
                red(nmax[0:64, 0:1], PS[0:64, 0:KEYS], AX.X, MAX, negate=True).then_inc(z_max, 1)
                dve.wait_ge(z_ln, b + 1)
                s = slice(64, 96)
                link(tt(T1[s], PS[s, 0:KEYS], T1[s], MAX))
                link(nc.vector.tensor_tensor_scan(T2[s, 1:KEYS + 1], onec[s].to_broadcast([32, KEYS]), T1[s], 0.0, MUL, ADD))
                link(tt(T1[s], PS[s, 0:KEYS], T2[s, 0:KEYS], ADD))
                ts(nmax[s, 0:1], T2[s, KEYS:KEYS + 1], -1.0, None, MUL).then_inc(z_sb, 1)
                dve.wait_ge(z_exp, 2 * b + 2)
                link(recip(rinv[0:64, 0:1], rsum[0:64, 0:1]))
                ts(Z[0:64, b % 2, :], Z[0:64, b % 2, :], rinv[0:64, 0:1], None, MUL).then_inc(pn_ready, 1)

            def take_turned_p(b):
                for jj in range(2):
                    dve.wait_ge(spt_ps, 2 * b + jj + 1)
                    if b and jj == 0:
                        dve.wait_ge(spv_ps, b)
                    if jj == 0:
                        copy(PTs[:, 0:5, :], PS[:, 7 * 512:7 * 512 + 480].rearrange("p (j r) -> p j r", j=5)).then_inc(spt_ev, 1)
                    else:
                        link(copy(PTs[:, 5:8, :], PS[:, 7 * 512:7 * 512 + 288].rearrange("p (j r) -> p j r", j=3)))
                        copy(PTs[0:NS, 8, :], PS[0:NS, 7 * 512 + 288:7 * 512 + 384]).then_inc(spt_ev, 1)

            spread_q(0)
            for b in range(DB + 1):
                if b + 1 < DB:
                    spread_q(b + 1)
                if b >= 1:
                    take_turned_p(b - 1)
                if b < DB:
                    sampled_softmax(b)

            dve.wait_ge(in_resid, 16 * 5)
            for n in range(10):
                g, t = divmod(n, 5)
                t0, nr = TILES[t]
                dve.wait_ge(o_ps, n + 1)
                x = x2[0:nr, t, g * 512:(g + 1) * 512]
                tt(x, x, PS[0:nr, (n % 8) * 512:(n % 8 + 1) * 512], ADD).then_inc(o_ev, 1)
            for i, (t0, nr) in enumerate(TILES):
                dve.wait_ge(x2_std, i + 1)
                link(recip(rstd[:, i:i + 1], rstd[:, i:i + 1]))
                ts(xs[0:nr, i, :], x2[0:nr, i, :], rstd[0:nr, i:i + 1], None, MUL).then_inc(x2s_ready, 1)
                if i >= 1:
                    dve.wait_ge(h2_ps, i)
                    take_turned(i - 1, h2T, C_MN, h2_ready)
            dve.wait_ge(h2_ps, 5)
            take_turned(4, h2T, C_MN, h2_ready)
            for n in range(32):
                dve.wait_ge(u_ev, n + 1)
                tt(uT[:, n, :], uT[:, n, :], uT[:, n, :], MUL).then_inc(u_sq, 1)
            for n in range(10):
                g, t = divmod(n, 5)
                t0, nr = TILES[t]
                dve.wait_ge(y_ps, n + 1)
                x = x2[0:nr, t, g * 512:(g + 1) * 512]
                tt(x, x, PS[0:nr, (n % 8) * 512:(n % 8 + 1) * 512], ADD).then_inc(y_ready, 1)


def take_y(nc, act, qt, mt_ps, mt_ev, mixT, PS):
    for n in range(2):
        act.wait_ge(mt_ps, 2 * qt + n + 1)
        nc.scalar.activation(mixT[:, 2 + 3 * n:5 + 3 * n, qt * 128:(qt + 1) * 128],
                             PS[:, 7 * 512:7 * 512 + 384].rearrange("p (j t) -> p j t", j=3), ACT.Copy).then_inc(mt_ev, 1)


def _channels(a, n):
    return np.ascontiguousarray(np.asarray(a).reshape(n, 128).T)


def kernel(**inputs):
    import concourse.bacc as bacc
    from concourse.bass_utils import run_bass_kernel_spmd

    v = {k: np.ascontiguousarray(a) for k, a in inputs.items()}
    cst, rc, sc = constants()
    prm = np.zeros((128, N_PRM), np.float32)
    for name, c, n in (("attn_norm", C_AN, 8), ("mlp_norm", C_MN, 8), ("rwkv_mu", C_MU, 8), ("rwkv_w0", C_W0, 2),
                       ("rwkv_a0", C_A0, 2), ("rwkv_k_k", C_KK, 2), ("rwkv_k_a", C_KA, 2), ("rwkv_r_k", C_RK, 2),
                       ("rwkv_gn_w", C_GW, 2), ("rwkv_gn_b", C_GB, 2), ("q_norm", C_QN, 4)):
        prm[:, c:c + n] = _channels(v[name], n)
    prm[:, C_QN + 4:C_QN + 6] = 1
    prm[:, C_BM:C_BM + DB] = (np.arange(128)[:, None] % 64 // DT == np.arange(DB)[None, :])
    prm[:, C_BF:C_BF + 4] = v["b_forget"]
    arrays = {n: v[n] for n in ("x_prompt", "x_sample", "cache_kv", "page_table", "w_in", "rwkv_g_up", "k_norm",
                                "w_out", "w_mlp_up", "w_mlp_down")}
    arrays["logf_t"] = np.ascontiguousarray(v["cache_logf"][0].transpose(0, 2, 1))
    arrays["lora_wa"] = np.concatenate([v["rwkv_w_up"][0], v["rwkv_a_up"][0]], axis=0)
    arrays["shift0"] = np.ascontiguousarray(v["state_shift"][0].reshape(DB, 8, 128).transpose(2, 1, 0).reshape(128, 64))
    arrays["s0"] = np.ascontiguousarray(v["state_wkv"][0].reshape(DB, 2, 2, HD, HD).transpose(2, 4, 1, 0, 3).reshape(128, 1024))
    arrays.update(cst=cst, rc=rc, sc=sc[:, 0:N_SC], prm=prm)
    arrays = {n: np.ascontiguousarray(a) for n, a in arrays.items()}
    outs = {"y_prompt": (SEQ, D), "y_sample": (NS, D), "kv_prompt": (SEQ, 2 * AW), "kv_sample": (NS, 2 * AW),
            "logf_prompt": (SEQ, 4), "logf_sample": (NS, 4), "wkv_prompt": (128, 128), "wkv_sample": (128, 1024),
            "shift_prompt": (1, N_RW), "shift_sample": (DB, N_RW)}

    nc = bacc.Bacc("TRN2", target_bir_lowering=False, num_devices=1)
    d = {n: nc.dram_tensor(f"in_{n}", a.shape, mybir.dt.from_np(a.dtype), kind="ExternalInput").ap()
         for n, a in arrays.items()}
    o = {n: nc.dram_tensor(f"out_{n}", s, F32, kind="ExternalOutput").ap() for n, s in outs.items()}
    build(nc, d, o)
    r = run_bass_kernel_spmd(nc, [{f"in_{n}": a for n, a in arrays.items()}], core_ids=[0]).results[0]
    g = {n: np.asarray(r[f"out_{n}"]) for n in outs}
    wkv_p = g["wkv_prompt"].reshape(2, HD, 2, HD).transpose(2, 0, 3, 1).reshape(1, 1, 4, HD, HD)
    wkv_s = g["wkv_sample"].reshape(2, HD, 2, DB, HD).transpose(3, 2, 0, 4, 1).reshape(1, DB, 4, HD, HD)
    return (g["y_prompt"].reshape(1, SEQ, D), g["y_sample"].reshape(DB, DT, D),
            g["kv_prompt"].reshape(1, 1, SEQ, 2, H_ATT, HD), g["kv_sample"].reshape(1, DB, DT, 2, H_ATT, HD),
            g["logf_prompt"].reshape(1, 1, SEQ, 4), g["logf_sample"].reshape(1, DB, DT, 4),
            np.ascontiguousarray(wkv_p), np.ascontiguousarray(wkv_s),
            g["shift_prompt"].reshape(1, 1, N_RW), g["shift_sample"].reshape(1, DB, N_RW))
```

```python
from contextlib import ExitStack

import numpy as np
import concourse.bass as bass
from concourse import mybir

F32 = mybir.dt.float32
I32 = mybir.dt.int32
ALU = mybir.AluOpType
ACT = mybir.ActivationFunctionType
AX = mybir.AxisListType

D = 1024
SEQ, DB, DT = 512, 8, 8
NS = DB * DT
T = SEQ + NS
PAST, PAGE = 1024, 128
NPG = PAST // PAGE
HD = 64
H_ATT = 12
AW = H_ATT * HD
N_RW = 1024
DFF = 4 * D
KT = D // 128
CH = 64
NCH = T // CH
TILES = [(i * 128, 128) for i in range(4)] + [(SEQ, NS)]
NEG = -1e30
SP_MAX = 30.0
RMS_EPS = 1e-6
GN_EPS = 64e-5
DECAY = -float(np.exp(-0.5))
KEYS = PAST + NS
BLK = 256
NBLK = PAST // BLK

C_AN, C_MN, C_MU, C_W0, C_A0, C_KK, C_KA, C_RK, C_GW, C_GB, C_QN = 0, 8, 16, 24, 26, 28, 30, 32, 34, 36, 38
C_BM = 44
C_BF = 52
N_PRM = 56
K_ID, K_ONE, K_CAU, K_STR, K_ID64 = 0, 128, 256, 384, 512
N_CST = 576
R_SU, R_IU, R_LEV, R_L1, R_L1T, R_BM = 0, 576, 1152, 1472, 1536, 1600
N_RC = 2112
S_MASK, S_HB, S_IOTA, S_QBD = 0, 512, 768, 772
N_SC = S_QBD
R_AHEAD, A_BESIDE = 12, 32
N_PC = 512 + 64


def constants():
    p = np.arange(128)
    cst = np.zeros((128, N_CST), np.float32)
    cst[:, K_ID:K_ID + 128] = np.eye(128)
    cst[:, K_ONE:K_ONE + 128] = (p[:, None] // 64 == p[None, :] // 64)
    cst[:, K_CAU:K_CAU + 128] = np.where(p[None, :] <= p[:, None], 0, NEG)
    cst[:, K_STR:K_STR + 128] = np.where(p[None, :] < p[:, None], 0, NEG)
    q = p % 64
    t = np.arange(64)
    cst[:, K_ID64:K_ID64 + 64] = (q[:, None] == t[None, :])
    rc = np.zeros((128, N_RC), np.float32)
    same = q[:, None] // DT == t[None, :] // DT
    for at, keep in ((R_SU, q[:, None] < t[None, :]), (R_IU, q[:, None] <= t[None, :])):
        for c in range(NCH):
            rc[:, at + c * CH:at + (c + 1) * CH] = keep if c < NCH - 1 else keep & same
    def level(a, b, m):
        return (a // (2 * m) == b // (2 * m)) & (a // m % 2 == 1) & (b // m % 2 == 0)
    for n, m in enumerate((2, 4, 8, 16, 32)):
        rc[:, R_LEV + n * 64:R_LEV + (n + 1) * 64] = level(t[None, :], q[:, None], m)
    rc[:, R_L1:R_L1 + 64] = level(q[:, None], t[None, :], 1)
    rc[:, R_L1T:R_L1T + 64] = level(t[None, :], q[:, None], 1)
    for b in range(DB):
        rc[:, R_BM + b * 64:R_BM + (b + 1) * 64] = (t // DT == b)
    sc = np.zeros((128, N_SC), np.float32)
    pcst = np.zeros((128, N_PC), np.float32)
    r = p % DT
    strict = (p // 32 == 2)
    for b in range(DB):
        own = t[None, :] // DT == b
        s = t[None, :] % DT
        ok = own & np.where(strict[:, None], s < r[:, None], s <= r[:, None])
        sc[:, S_MASK + b * 64:S_MASK + (b + 1) * 64] = np.where(ok, 0, NEG)
    for h in range(4):
        pcst[h, h * 128:(h + 1) * 128] = -1
    for b in range(DB):
        for h in range(4):
            sc[4 * b + h, S_HB + 32 * b + 8 * h:S_HB + 32 * b + 8 * h + 8] = -1
            pcst[4 * b + h, 512:576] = (t // DT == b)
    sc[:, S_IOTA:S_IOTA + 4] = np.arange(1, 5)
    return cst, rc, sc, pcst


def build(nc, d, o):
    ctx = ExitStack()
    with ctx:
        def sb(name, shape, dt=F32):
            return ctx.enter_context(nc.sbuf_tensor(name, shape, dt))

        def sem(name):
            return ctx.enter_context(nc.semaphore(name))

        cst = sb("cst", [128, N_CST])
        rc = sb("rc", [128, N_RC])
        prm = sb("prm", [128, N_PRM])
        NW = 3
        W = sb("W", [128, NW, 4096])
        HM = sb("HM", [128, 8, T])
        QK = sb("QK", [128, 12, T])
        VQ = sb("VQ", [128, 7680])
        AR = sb("AR", [128, 16, 2 * T])
        small = sb("small", [128, 264])
        pt_sb = sb("pt_sb", [1, DB * NPG], I32)
        PS = ctx.enter_context(nc.psum_tensor("PS", [128, 8 * 512], F32))

        ident = cst[:, K_ID:K_ID + 128]
        ones_head = cst[:, K_ONE:K_ONE + 128]
        hT = HM
        mixT = HM
        qT, kT = QK[:, 0:6, :], QK[:, 6:12, :]
        h2T = QK[:, 0:8, :]
        xin = VQ[:, 0:5 * D].rearrange("p (t c) -> p t c", t=5)
        V = VQ[:, 0:5 * AW].rearrange("p (t c) -> p t c", t=5)
        ring = VQ[:, 5 * AW:].rearrange("p (g t c) -> p g t c", g=2, t=5)
        x2 = xin

        Wf = W[:, :, :].rearrange("p a c -> p (a c)")

        def slot(n):
            if n >= 17:
                return Wf[:, (n - 17) * 2 * T:(n - 16) * 2 * T].rearrange("p (a t) -> p a t", a=2)
            return AR[:, n, :].rearrange("p (a t) -> p a t", a=2)

        def chunked(n):
            return slot(n).rearrange("p a (c s) -> p a c s", s=CH)

        ARf = AR[:, :, :].rearrange("p a c -> p (a c)")
        pT = ARf[:, 0:8 * T].rearrange("p (a t) -> p a t", a=8)
        xm = ARf[:, 8 * T:16 * T].rearrange("p (a t) -> p a t", a=8)
        xs = ARf[:, 16 * T:16 * T + 5 * D].rearrange("p (t c) -> p t c", t=5)
        reset = AR[:, 14, 0:T]
        knorm = AR[:, 14, T:T + 512]
        sqtmp = AR[:, 15, :].rearrange("p (g c) -> p g c", g=3)
        lora = AR[:, 12, 0:512]
        shift_sb = AR[0:9, 13, 0:N_RW]
        shift0 = small[:, 128:192].rearrange("p (m b) -> p m b", m=8)
        ssq = small[:, 0:5]
        rstd = small[:, 5:10]
        eps = small[:, 10:11]
        gneps = small[:, 11:12]
        omka = small[:, 12:14]
        qss = small[:, 16:46].rearrange("p (t h) -> p t h", t=5)
        qrs = small[:, 46:76].rearrange("p (t h) -> p t h", t=5)
        logf = small[:, 76:96]
        ftmp = small[:, 96:116]
        gq = small[:, 116:122]
        nmax = small[:, 192:200]
        rsum = small[:, 200:208]
        rinv = small[:, 208:216]
        gate = small[:, 216:220]
        gsel = small[:, 220:224]
        gmin = small[:, 224:226]
        onec = small[:, 226:227]
        lfx = small[0:NS, 228:260]
        pc = sb("pc", [128, 2, 16])

        X4 = VQ[:, 5 * AW:]
        S0 = X4[:, 0:1024].rearrange("p (a b i) -> p a b i", a=2, b=DB)
        hexp = X4[:, 1024:2048].rearrange("p (a b i) -> p a b i", a=2, b=DB)
        uexp = AR[:, 7, 0:1024].rearrange("p (a b i) -> p a b i", a=2, b=DB)
        sfin = X4[:, 3648:3776].rearrange("p (a i) -> p a i", a=2)

        NKR = 4
        Kr = ARf[:, 0:NKR * AW].rearrange("p (r c) -> p r c", r=NKR)
        Vr = ARf[:, NKR * AW:(NKR + NPG) * AW].rearrange("p (r c) -> p r c", r=NPG)
        at0 = (NKR + NPG) * AW
        Call = X4[0:32, 2048:2048 + KEYS]
        cT = X4[0:4, 3136:3136 + SEQ]
        qbd = rc[:, S_QBD:S_QBD + 384].rearrange("p (g c q) -> p g c q", g=2, c=6)
        NP_ = 5
        w0 = 3 * 2 * T

        def wpart(n, shape_str=None, **kw):
            nonlocal w0
            ap = Wf[:, w0:w0 + n]
            w0 += n
            return ap.rearrange(shape_str, **kw) if shape_str else ap

        cb = wpart(4 * SEQ, "p (h k) -> p h k", h=4)
        P4 = wpart(4 * 512, "p (r k) -> p r k", r=4)
        Pp = [P4[:, r, :] for r in range(4)] + [X4[:, 3136:3648]]
        PTp = wpart(2 * 512, "p (r k) -> p r k", r=2)
        Ya = wpart(2 * AW, "p (r k) -> p r k", r=2)
        T1p = wpart(2 * 512, "p (r k) -> p r k", r=2)
        T2p = wpart(520)
        hot = wpart(512)
        own = wpart(NS)
        assert w0 <= NW * 4096
        KTb = ARf[:, at0:at0 + 3072].rearrange("p (g c k) -> p g c k", g=2, c=6)
        Z = ARf[0:96, at0 + 3072:at0 + 3072 + 2 * KEYS].rearrange("p (g k) -> p g k", g=2)
        T1 = ARf[0:96, at0 + 5248:at0 + 5248 + KEYS]
        T2 = ARf[0:96, at0 + 6336:at0 + 6336 + KEYS + 4]
        PTs = ARf[:, at0 + 7500:at0 + 7500 + 9 * 96].rearrange("p (k r) -> p k r", k=9)
        Ys = ARf[0:96, at0 + 8364:at0 + 8364 + 256]
        assert at0 + 8364 + 256 <= 16 * 2 * T

        uT = ARf[:, :].rearrange("p (f t) -> p f t", f=32)

        in_const = sem("in_const")
        in_resid = sem("in_resid")
        in_rc = sem("in_rc")
        in_sc = sem("in_sc")
        in_pc = sem("in_pc")
        in_s0 = sem("in_s0")
        in_lf = sem("in_lf")
        in_lora = sem("in_lora")
        in_kn = sem("in_kn")
        dn_used = sem("dn_used")
        y_stored = sem("y_stored")
        stored = sem("stored")
        v_step = sem("v_step")
        a_step = sem("a_step")
        init = sem("init")
        squares = sem("squares")
        std_ready = sem("std_ready")
        xs_ready = sem("xs_ready")
        xT_ps = sem("xT_ps")
        hT_ready = sem("hT_ready")
        p_ps = sem("p_ps")
        p_ready = sem("p_ready")
        qkv_ps = sem("qkv_ps")
        qkv_ev = sem("qkv_ev")
        sq_ready = sem("sq_ready")
        sq_used = sem("sq_used")
        qstd_ready = sem("qstd_ready")
        qk_normed = sem("qk_normed")
        tr_ps = sem("tr_ps")
        tr_ev = sem("tr_ev")
        k_out = sem("k_out")
        xm_ready = sem("xm_ready")
        shift_ps = sem("shift_ps")
        shift_ev = sem("shift_ev")
        shift_out = sem("shift_out")
        lact = sem("lact")
        lora_ps = sem("lora_ps")
        lora_ev = sem("lora_ev")
        kksq_ready = sem("kksq_ready")
        hs_ps = sem("hs_ps")
        hs_ev = sem("hs_ev")
        kkstd_ready = sem("kkstd_ready")
        bonus_in = sem("bonus_in")
        exp_in = sem("exp_in")
        exp_out = sem("exp_out")
        ops_ready = sem("ops_ready")
        c_ps = sem("c_ps")
        c_ev = sem("c_ev")
        ltm_ready = sem("ltm_ready")
        masked_ready = sem("masked_ready")
        logf_in = sem("logf_in")
        logf_a = sem("logf_a")
        logf_ready = sem("logf_ready")
        gnstd_ready = sem("gnstd_ready")
        rw_done = sem("rw_done")
        s1_ready = sem("s1_ready")
        lt_ps = sem("lt_ps")
        lfx_ready = sem("lfx_ready")
        cT_ready = sem("cT_ready")
        lfn_ready = sem("lfn_ready")
        cb_ps = sem("cb_ps")
        cb_ready = sem("cb_ready")
        s_ps = sem("s_ps")
        s_ev = sem("s_ev")
        a_in = sem("a_in")
        a_mid = sem("a_mid")
        sb_in = sem("sb_in")
        p_out = sem("p_out")
        pt_ps = sem("pt_ps")
        pt_ev = sem("pt_ev")
        pv_ps = sem("pv_ps")
        pv_ev = sem("pv_ev")
        mt_ps = sem("mt_ps")
        mt_ev = sem("mt_ev")
        kt_ps = sem("kt_ps")
        kt_ev = sem("kt_ev")
        sg_ps = sem("sg_ps")
        ss_ps = sem("ss_ps")
        qbd_ready = sem("qbd_ready")
        call_ready = sem("call_ready")
        z_old = sem("z_old")
        z_new = sem("z_new")
        z_abs = sem("z_abs")
        z_ln = sem("z_ln")
        z_max = sem("z_max")
        z_sb = sem("z_sb")
        z_exp = sem("z_exp")
        pn_ready = sem("pn_ready")
        spt_ps = sem("spt_ps")
        spt_ev = sem("spt_ev")
        spv_ps = sem("spv_ps")
        spv_ev = sem("spv_ev")
        ys_ready = sem("ys_ready")
        yt_ps = sem("yt_ps")
        o_ps = sem("o_ps")
        o_ev = sem("o_ev")
        x2_ssq = sem("x2_ssq")
        x2_std = sem("x2_std")
        x2s_ready = sem("x2s_ready")
        h2_ps = sem("h2_ps")
        h2_ready = sem("h2_ready")
        u_ps = sem("u_ps")
        u_ev = sem("u_ev")
        u_sq = sem("u_sq")
        y_ps = sem("y_ps")
        y_ready = sem("y_ready")
        in_x = [sem(f"in_x{i}") for i in range(5)]
        in_w = [sem(f"in_w{i}") for i in range(NW)]
        in_k = [sem(f"in_k{i}") for i in range(NKR)]
        in_v = [sem(f"in_v{i}") for i in range(NPG)]
        w_in = d["w_in"][0].rearrange("(k p) c -> p k c", p=128)
        w_out = d["w_out"][0].rearrange("(k p) c -> p k c", p=128)
        w_up = d["w_mlp_up"][0].rearrange("(k p) c -> p k c", p=128)
        w_dn = d["w_mlp_down"][0].rearrange("(k p) c -> p k c", p=128)
        QC = 384
        QW = [QC] * 5 + [QC + 4]
        pieces = [w_in[:, :, g * 512:(g + 1) * 512] for g in range(2)]
        pieces += [w_in[:, :, N_RW + g * QC:N_RW + g * QC + QW[g]] for g in range(6)]
        P_OUT = len(pieces)
        pieces += [w_out[:, :, g * 512:(g + 1) * 512] for g in range(2)]
        P_UP = len(pieces)
        pieces += [w_up[:, :, g * 512:(g + 1) * 512] for g in range(8)]
        P_DN = len(pieces)
        pieces += [w_dn[:, g * 8:(g + 1) * 8, n * 512:(n + 1) * 512] for n in range(2) for g in range(4)]

        def wview(n):
            cols = pieces[n].shape[2]
            return W[:, n % NW, 0:8 * cols].rearrange("p (k c) -> p k c", k=8)

        def w_wait(eng, n):
            eng.wait_ge(in_w[n % NW], 16 * (n // NW + 1))

        def used(n):
            if n < 2:
                return p_ps, 4 * (n + 1)
            if n < P_OUT:
                return qkv_ps, 5 * (n - 1)
            if n < P_UP:
                return o_ps, 5 * (n - P_OUT + 1)
            if n < P_DN:
                return u_ps, 4 * (n - P_UP + 1)
            half, g = divmod(n - P_DN, 4)
            return (dn_used, 3 * half + g + 1) if g < 3 else (y_ps, 5 * (half + 1))

        def xrows(i):
            t0, nr = TILES[i]
            return d["x_prompt"][0, t0:t0 + nr, :] if i < 4 else d["x_sample"].rearrange("b t c -> (b t) c")

        def orows(name, i, c0, c1):
            t0, nr = TILES[i]
            if i < 4:
                return o[name + "_prompt"][t0:t0 + nr, c0:c1]
            return o[name + "_sample"][:, c0:c1]

        def pair(n, width=2 * 288):
            return PS[:, n * 1024:(n + 1) * 1024].rearrange("p (a t) -> p a t", a=2)[:, :, 0:width // 2]

        def page_at(eng, n):
            return bass.ds(eng.value_load(pt_sb[0:1, n:n + 1], min_val=0, max_val=d["cache_kv"].shape[1] - 1), 1)

        def halves(ap):
            return ap.rearrange("p (a t) -> p a t", a=2)

        STEPS = [(k, a) for k in ("LT", "L", "ArbT", "LkT", "ArkT", "Vt", "KQt", "BEt", "KEt") for a in (0, 1)]
        for lev in range(5):
            STEPS += [(f"{k}{lev}", a) for k in (("W", "dX", "dXT") if lev < 4 else ("W", "dXT")) for a in (0, 1)]
        STEPS += [(k, a) for k in ("T1", "HT", "H", "G", "MT", "N") for a in (0, 1)]
        STEPS += [(f"seq{c}", 0) for c in range(1, 8)]
        STEPS += [(k, a) for k in ("U", "Y", "SS", "GM", "GV") for a in (0, 1)]
        AT = {s: n for n, s in enumerate(STEPS)}

        UNITS = [(qt, h) for qt in range(4) for h in range(H_ATT)]
        NU = len(UNITS)

        def is_sb(u):
            return 0 <= u < NU and UNITS[u][1] >= 8

        NA = NU + 9
        ORDER = []
        for n in range(len(STEPS)):
            ORDER.append(("R", n))
            if n in (1, 5, 9):
                ORDER.append(("L", (n - 1) // 4))
            elif n >= R_AHEAD:
                done = (n - R_AHEAD + 1) * A_BESIDE // (len(STEPS) - R_AHEAD)
                ORDER += [("A", i) for i in range((n - R_AHEAD) * A_BESIDE // (len(STEPS) - R_AHEAD), done)]
        ORDER += [("G", 0), ("A", done), ("A", done + 1), ("G", 1)] + [("A", i) for i in range(done + 2, NA)]

        block = ctx.enter_context(nc.Block())

        @block.sync
        def _(sp):
            for i, (t0, nr) in enumerate(TILES):
                sp.dma_start(xin[0:nr, i, :], xrows(i)).then_inc(in_x[i], 16)
            sp.dma_start(cst[:, :], d["cst"]).then_inc(in_const, 16)
            sp.dma_start(prm[:, :], d["prm"]).then_inc(in_const, 16)
            sp.dma_start(small[:, 128:192], d["shift0"]).then_inc(in_const, 16)
            sp.dma_start(pt_sb[:, :], d["page_table"].rearrange("(o b) n -> o (b n)", o=1)).then_inc(in_const, 16)
            sp.dma_start(rc[:, :], d["rc"]).then_inc(in_rc, 16)

            def load_w(n):
                if n >= NW:
                    sp.wait_ge(*used(n - NW))
                sp.dma_start(wview(n), pieces[n]).then_inc(in_w[n % NW], 16)

            for n in range(NW):
                load_w(n)
            sp.wait_ge(xT_ps, 5)
            sp.dma_start(lora[:, 0:256], d["lora_wa"]).then_inc(in_lora, 16)
            sp.dma_start(lora[:, 256:512], d["rwkv_g_up"][0]).then_inc(in_lora, 16)
            sp.dma_start(knorm, d["k_norm"].rearrange("l h d -> l (h d)").to_broadcast([128, 512])).then_inc(in_kn, 16)
            for n in range(NW, P_OUT):
                load_w(n)
            sp.wait_ge(qkv_ps, 30)
            sp.dma_start(Wf[:, w0 - N_PC:w0], d["pcst"]).then_inc(in_pc, 16)
            sp.wait_ge(tr_ps, 20)
            sp.wait_ge(k_out, 16 * 10)
            sp.dma_start(X4[:, 0:1024], d["s0"]).then_inc(in_s0, 16)
            sp.wait_ge(in_const, 16 * 4)
            for n in range(DB * NPG):
                b, p = divmod(n, NPG)
                sp.dma_start(Call[4 * b:4 * b + 4, p * PAGE:(p + 1) * PAGE],
                             d["logf_t"][page_at(sp, n), :, :].rearrange("n h t -> (n h) t")).then_inc(in_lf, 16)

            def load_k(n):
                src = d["cache_kv"][0, page_at(sp, n), :, 0, :, :].rearrange("n t h c -> (n t) (h c)")
                if n >= NKR:
                    sp.wait_ge(kt_ps, 2 * (n - NKR + 1))
                sp.dma_start(Kr[:, n % NKR, :], src).then_inc(in_k[n % NKR], 16)

            sp.wait_ge(c_ps, AT["U", 1] + 1)
            for n in range(NKR):
                load_k(n)
            sp.wait_ge(rw_done, 1)
            sp.dma_start(rc[:, 0:N_SC], d["sc"]).then_inc(in_sc, 16)
            for n in range(NKR, DB * NPG):
                load_k(n)
                if n == 2 * NPG:
                    sp.wait_ge(mt_ps, 8)
                    for m in range(P_OUT, P_OUT + NW):
                        load_w(m)
            sp.wait_ge(spv_ps, DB)
            sp.wait_ge(stored, 16 * 12)
            for i, (t0, nr) in enumerate(TILES):
                sp.dma_start(x2[0:nr, i, :], xrows(i)).then_inc(in_resid, 16)
            for n in range(P_OUT + NW, len(pieces)):
                load_w(n)
            for i, (t0, nr) in enumerate(TILES):
                sp.wait_ge(y_ready, 6 + i)
                sp.dma_start(orows("y", i, 0, D), x2[0:nr, i, :]).then_inc(y_stored, 16)
            sp.wait_ge(y_stored, 16 * 5)
            sp.wait_ge(stored, 16 * (5 + 5 + 2))
            sp.wait_ge(k_out, 16 * 10)
            sp.wait_ge(shift_out, 16 * 2)

        @block.gpsimd
        def _(pool):
            pool.wait_ge(shift_ev, 1)
            pool.dma_start(o["shift_prompt"], shift_sb[0:1, :]).then_inc(shift_out, 16)
            pool.dma_start(o["shift_sample"], shift_sb[1:9, :]).then_inc(shift_out, 16)
            for g in (2, 3):
                pool.wait_ge(qk_normed, 5 * (g + 1))
                for i, (t0, nr) in enumerate(TILES):
                    c0 = (g - 2) * QC
                    pool.dma_start(orows("kv", i, c0, c0 + QC), ring[0:nr, g % 2, i, :]).then_inc(k_out, 16)
            pool.wait_ge(qkv_ev, 30)
            for i, (t0, nr) in enumerate(TILES):
                pool.dma_start(orows("kv", i, AW, 2 * AW), V[0:nr, i, :]).then_inc(stored, 16)
            pool.wait_ge(logf_ready, 1)
            for i, (t0, nr) in enumerate(TILES):
                pool.dma_start(orows("logf", i, 0, 4), logf[0:nr, 4 * i:4 * i + 4]).then_inc(stored, 16)
            pool.wait_ge(rw_done, 1)
            pool.dma_start(o["wkv_prompt"], X4[:, 3648:3776]).then_inc(stored, 16)
            pool.dma_start(o["wkv_sample"], X4[:, 0:1024]).then_inc(stored, 16)
            pool.wait_ge(in_const, 16 * 4)
            for n in range(DB * NPG):
                src = d["cache_kv"][0, page_at(pool, n), :, 1, :, :].rearrange("n t h c -> (n t) (h c)")
                if n >= NPG:
                    pool.wait_ge(spv_ps, n // NPG)
                pool.dma_start(Vr[:, n % NPG, :], src).then_inc(in_v[n % NPG], 16)

        @block.tensor
        def _(pe):
            mm, turn = nc.tensor.matmul, nc.tensor.transpose

            pe.wait_ge(in_const, 16 * 4)
            for i, (t0, nr) in enumerate(TILES):
                pe.wait_ge(xs_ready, i + 1)
                if i >= 2:
                    pe.wait_ge(hT_ready, i - 1)
                base = (i % 2) * 1024
                for k in range(KT):
                    last = turn(PS[:, base + k * 128:base + k * 128 + nr], xs[0:nr, i, k * 128:(k + 1) * 128],
                                ident[0:nr, 0:nr])
                last.then_inc(xT_ps, 1)

            pe.wait_ge(hT_ready, 5)
            for m in range(8):
                w_wait(pe, m // 4)
                if m >= 4:
                    pe.wait_ge(p_ready, m - 3)
                out = pair(m % 4)
                for k in range(KT):
                    for a in range(2):
                        last = mm(out[:, a, :], wview(m // 4)[:, k, (m % 4) * 128:(m % 4 + 1) * 128],
                                  hT[:, k, a * 288:(a + 1) * 288], start=(k == 0), stop=(k == KT - 1))
                last.then_inc(p_ps, 1)

            def gemm(g):
                w_wait(pe, 2 + g)
                for t, (t0, nr) in enumerate(TILES):
                    n = g * 5 + t
                    if n >= 4:
                        pe.wait_ge(qkv_ev, n - 3)
                    for k in range(KT):
                        last = mm(PS[0:nr, (n % 4) * 512:(n % 4) * 512 + QW[g]], hT[:, k, t0:t0 + nr],
                                  wview(2 + g)[:, k, :], start=(k == 0), stop=(k == KT - 1))
                    last.then_inc(qkv_ps, 1)

            def turn_qk(g):
                for t, (t0, nr) in enumerate(TILES):
                    r = g * 5 + t
                    pe.wait_ge(qk_normed, r + 1)
                    if r >= 2:
                        pe.wait_ge(tr_ev, r - 1)
                    base = (6 + r % 2) * 512
                    for j in range(3):
                        last = turn(PS[:, base + j * 128:base + j * 128 + nr],
                                    ring[0:nr, g % 2, t, j * 128:(j + 1) * 128], ident[0:nr, 0:nr])
                    last.then_inc(tr_ps, 1)

            def head_sums(j0, slot_n):
                for a in range(2):
                    j = j0 + a
                    if j >= 2:
                        pe.wait_ge(hs_ev, j - 1)
                    src = slot(slot_n)[:, a, :]
                    for hf in range(2):
                        last = mm(pair(2 + j % 2)[:, hf, :], ones_head, src[:, hf * 288:(hf + 1) * 288], start=True, stop=True)
                    last.then_inc(hs_ps, 1)

            pe.wait_ge(p_ready, 8)
            for m in range(8):
                last = turn(PS[0:9, 2048 + m * 128:2048 + (m + 1) * 128], pT[:, m, SEQ - 1:T:DT], ident)
            last.then_inc(shift_ps, 1)
            gemm(0)
            gemm(1)
            pe.wait_ge(lact, 2)
            pe.wait_ge(in_lora, 32)
            pe.wait_ge(shift_ev, 1)
            for j in range(6):
                if j >= 2:
                    pe.wait_ge(lora_ev, j - 1)
                rows = (slice(0, 64), slice(64, 128), slice(0, 128))[j // 2]
                lhs = lora[rows, (0, 0, 256)[j // 2] + (j % 2) * 128:][:, 0:128]
                for hf in range(2):
                    last = mm(pair(2 + j % 2)[:, hf, :], lhs, xm[rows, (6, 6, 7)[j // 2], hf * 288:(hf + 1) * 288],
                              start=True, stop=True)
                last.then_inc(lora_ps, 1)
            pe.wait_ge(lora_ev, 6)
            turn_qk(0)
            gemm(2)
            pe.wait_ge(kksq_ready, 1)
            pe.wait_ge(tr_ev, 5)
            head_sums(0, 12)
            pe.wait_ge(bonus_in, 1)
            head_sums(2, 13)
            pe.wait_ge(hs_ev, 4)
            turn_qk(1)
            gemm(3)
            turn_qk(2)
            gemm(4)
            turn_qk(3)
            gemm(5)

            pe.wait_ge(ops_ready, 1)
            pe.wait_ge(qkv_ev, 30)
            pe.wait_ge(tr_ev, 20)
            pe.wait_ge(hs_ev, 4)

            def begin(kind, a, *after):
                n = AT[kind, a]
                need = max([AT[x, a] + 1 for x in after] + ([n - 1] if n >= 2 else []), default=0)
                if need:
                    pe.wait_ge(c_ev, need)
                return (n % 2) * 1024

            def per_chunk(base, a, A, B, chunks=range(NCH), start=True, stop=True):
                for c in chunks:
                    for h in (slice(0, 64), slice(64, 128)):
                        last = mm(PS[h, base + c * CH:base + (c + 1) * CH], chunked(A)[h, a, c, :],
                                  B(h, a, c) if callable(B) else chunked(B)[h, a, c, :], start=start, stop=stop)
                return last

            def eye(h, a, c):
                return cst[h, K_ID:K_ID + 128][:, h]

            def rwkv_products():
                for kind, A, B in (("LT", 8, 1), ("L", 1, 8), ("ArbT", 8, 4), ("LkT", 3, 1), ("ArkT", 3, 4),
                                   ("Vt", 6, eye), ("KQt", 1, eye), ("BEt", 9, eye), ("KEt", 5, eye)):
                    for a in range(2):
                        base = begin(kind, a)
                        per_chunk(base, a, A, B).then_inc(c_ps, 1)
                        yield
                for lev in range(5):
                    for a in range(2):
                        base = begin(f"W{lev}", a, "L" if lev == 0 else f"dX{lev - 1}", "KEt")
                        pe.wait_ge(ltm_ready, 2 * lev + a + 1)
                        per_chunk(base, a, 3, 2).then_inc(c_ps, 1)
                        yield
                    if lev < 4:
                        for a in range(2):
                            base = begin(f"dX{lev}", a, f"W{lev}")
                            per_chunk(base, a, 8, 5).then_inc(c_ps, 1)
                            yield
                    for a in range(2):
                        base = begin(f"dXT{lev}", a, f"W{lev}")
                        per_chunk(base, a, 5, 8).then_inc(c_ps, 1)
                        yield
                for kind, A, B, after in (("T1", 7, 14, ()), ("HT", 15, 8, ("dXT4",)), ("H", 8, 15, ()), ("G", 8, 9, ("T1",))):
                    for a in range(2):
                        base = begin(kind, a, *after)
                        per_chunk(base, a, A, B).then_inc(c_ps, 1)
                        yield
                for a in range(2):
                    base = begin("MT", a, "H")
                    per_chunk(base, a, 1, 17, range(8)).then_inc(c_ps, 1)
                    yield
                for a in range(2):
                    base = begin("N", a, "G")
                    for c in range(8):
                        per_chunk(base, a, 18, 14, [c], stop=False)
                        last = per_chunk(base, a, 17, 19, [c], start=False)
                    last.then_inc(c_ps, 1)
                    yield
                pe.wait_ge(s1_ready, 1)
                for c in range(1, 8):
                    n = AT[f"seq{c}", 0]
                    pe.wait_ge(c_ev, n)
                    for a in range(2):
                        for h in (slice(0, 64), slice(64, 128)):
                            last = mm(PS[h, (n % 2) * 1024 + a * 64:(n % 2) * 1024 + (a + 1) * 64],
                                      chunked(2)[h, a, c, :], chunked(5)[h, a, c, :], start=True, stop=True)
                    last.then_inc(c_ps, 1)
                    yield
                pe.wait_ge(masked_ready, 2)
                pe.wait_ge(in_s0, 16)
                for a in range(2):
                    base = begin("U", a)
                    pe.wait_ge(c_ev, AT["seq7", 0] + 1)
                    per_chunk(base, a, 0, 5, range(1, 8))
                    for h in (slice(0, 64), slice(64, 128)):
                        for b in range(DB):
                            last = mm(PS[h, base + 8 * CH:base + 9 * CH], hexp[h, a, b, :], S0[h, a, b, :],
                                      start=(b == 0), stop=(b == DB - 1))
                    last.then_inc(c_ps, 1)
                    yield
                for a in range(2):
                    base = begin("Y", a, "U")
                    for c in range(NCH):
                        per_chunk(base, a, 9, 11, [c], stop=False)
                        if 1 <= c < 8:
                            per_chunk(base, a, 5, 4, [c], start=False, stop=False)
                        if c == 8:
                            for h in (slice(0, 64), slice(64, 128)):
                                for b in range(DB):
                                    c0 = SEQ + b * DT
                                    mm(PS[h, base + c0:base + c0 + DT], S0[h, a, b, :], slot(4)[h, a, c0:c0 + DT],
                                       start=False, stop=False, skip_group_check=True)
                        last = per_chunk(base, a, 14, 12, [c], start=False)
                    last.then_inc(c_ps, 1)
                    yield
                pe.wait_ge(masked_ready, 4)
                for a in range(2):
                    base = begin("SS", a)
                    for h in (slice(0, 64), slice(64, 128)):
                        mm(PS[h, base:base + 512], chunked(17)[h, a, 8, :], uexp[h, a, :, :], start=True, stop=False)
                        last = mm(PS[h, base:base + 512], chunked(18)[h, a, 8, :], hexp[h, a, :, :], start=False, stop=True)
                    last.then_inc(c_ps, 1)
                    yield
                for kind, src, after in (("GM", 6, "Y"), ("GV", 3, "GM")):
                    for a in range(2):
                        begin(kind, a, after)
                        out = pair(AT[kind, a] % 2)
                        for hf in range(2):
                            last = mm(out[:, hf, :], ones_head, slot(src)[:, a, hf * 288:(hf + 1) * 288], start=True, stop=True)
                        last.then_inc(c_ps, 1)
                        yield

            def log_sums(n):
                if n == 1:
                    pe.wait_ge(logf_ready, 1)
                    for i in range(4):
                        turn(PS[0:4, 2048 + i * 128:2048 + (i + 1) * 128], logf[:, 4 * i:4 * i + 4], ident)
                    pe.wait_ge(lfx_ready, 1)
                    mm(PS[0:32, 2560:2560 + NS], lfx, ident[0:NS, 0:NS], start=True, stop=True).then_inc(lt_ps, 1)
                if n == 2:
                    pe.wait_ge(cT_ready, 1)
                    pe.wait_ge(lfn_ready, 1)
                    pe.wait_ge(in_pc, 16)
                    for h in range(4):
                        mm(PS[:, (4 + h) * 512:(5 + h) * 512], hot[0:4, h * 128:(h + 1) * 128], cT,
                           start=True, stop=True).then_inc(cb_ps, 1)

            def scores(u):
                qt, h = UNITS[u]
                nk = (qt + 1) * 128
                if u >= 2:
                    pe.wait_ge(s_ev, u - 1)
                rows = slice(64 * (h % 2), 64 * (h % 2) + 64)
                mm(PS[:, (4 + u % 2) * 512:(4 + u % 2) * 512 + nk], qT[rows, h // 2, qt * 128:(qt + 1) * 128],
                   kT[rows, h // 2, 0:nk], start=True, stop=True).then_inc(s_ps, 1)

            def turn_p(u):
                qt, h = UNITS[u]
                pe.wait_ge(p_out, u + 1)
                if u >= 1:
                    pe.wait_ge(pt_ev, u)
                base = 6 * 512
                for j in range(qt + 1):
                    last = turn(PS[:, base + j * 128:base + (j + 1) * 128], Pp[u % NP_][:, j * 128:(j + 1) * 128], ident)
                last.then_inc(pt_ps, 1)

            def times_v(u):
                qt, h = UNITS[u]
                pe.wait_ge(pt_ev, u + 1)
                if u >= 1:
                    pe.wait_ge(pv_ev, u)
                c0 = 7 * 512
                for j in range(qt + 1):
                    last = mm(PS[:, c0:c0 + 64], PTp[:, u % 2, j * 128:(j + 1) * 128], V[:, j, h * HD:(h + 1) * HD],
                              start=(j == 0), stop=(j == qt))
                last.then_inc(pv_ps, 1)

            def turn_y(qt):
                pe.wait_ge(pv_ev, min(12 * (qt + 1) + 1, NU))
                for n in range(2):
                    if 2 * qt + n:
                        pe.wait_ge(mt_ev, 2 * qt + n)
                    for j in range(3):
                        c0 = (3 * n + j) * 128
                        last = turn(PS[:, 7 * 512 + j * 128:7 * 512 + (j + 1) * 128], Ya[:, qt % 2, c0:c0 + 128], ident)
                    last.then_inc(mt_ps, 1)

            rwkv = rwkv_products()
            for what, i in ORDER:
                if what == "R":
                    next(rwkv)
                elif what == "L":
                    log_sums(i)
                elif what == "A":
                    if i == 0:
                        pe.wait_ge(cb_ready, 4)
                    if i >= 20 and (i - 20) % 12 == 0:
                        turn_y((i - 20) // 12)
                        pe.wait_ge(mt_ev, 2 * ((i - 20) // 12 + 1))
                    if 0 <= i - 7 < NU:
                        times_v(i - 7)
                    if i < NU:
                        scores(i)
                    if 0 <= i - 5 < NU:
                        turn_p(i - 5)

            def turn_pages(b, g):
                for n in (b * NPG + 2 * g, b * NPG + 2 * g + 1):
                    pe.wait_ge(in_k[n % NKR], 16 * (n // NKR + 1))
                    for q in range(2):
                        m = 2 * n + q
                        if m >= 3:
                            pe.wait_ge(kt_ev, m - 2)
                        base = (3 + m % 3) * 512
                        for c in range(3):
                            last = turn(PS[:, base + c * 128:base + (c + 1) * 128],
                                        Kr[:, n % NKR, (3 * q + c) * 128:(3 * q + c + 1) * 128], ident)
                        last.then_inc(kt_ps, 1)

            def sampled_scores(b):
                turn_pages(b, 0)
                if b >= 1:
                    pe.wait_ge(z_old, b)
                    pe.wait_ge(z_new, b)
                if b >= 2:
                    turn_result(b - 2)
                pe.wait_ge(qbd_ready, b + 1)
                for g in range(NPG // 2):
                    if g + 1 < NPG // 2:
                        turn_pages(b, g + 1)
                    pe.wait_ge(kt_ev, 2 * (b * NPG + 2 * g + 2))
                    n = b * NPG // 2 + g
                    for k in range(2):
                        for x in range(3):
                            mm(PS[32 * x:32 * x + 32, g * 256:(g + 1) * 256], qbd[:, b % 2, 2 * x + k, :],
                               KTb[:, n % 2, 2 * x + k, :], start=(k == 0), stop=(k == 1 and x > 0))
                    if b == 0 and g == 0:
                        pe.wait_ge(call_ready, 1)
                    mm(PS[0:32, g * 256:(g + 1) * 256], rc[0:32, S_HB + 32 * b:S_HB + 32 * b + 32],
                       Call[:, g * 256:(g + 1) * 256], start=False, stop=True).then_inc(sg_ps, 1)
                for k in range(2):
                    for x in range(3):
                        mm(PS[32 * x:32 * x + 32, PAST:KEYS], qbd[:, b % 2, 2 * x + k, :],
                           kT[:, 2 * x + k, SEQ:T], start=(k == 0), stop=(k == 1 and x > 0))
                mm(PS[0:32, PAST:KEYS], rc[0:32, S_HB + 32 * b:S_HB + 32 * b + 32], Call[:, PAST:KEYS],
                   start=False, stop=True).then_inc(ss_ps, 1)

            def sampled_values(b):
                pe.wait_ge(pn_ready, b + 1)
                for jj in range(2):
                    n = 2 * b + jj
                    if n:
                        pe.wait_ge(spt_ev, n)
                    for j in range(5 * jj, min(5 * jj + 5, 9)):
                        nk = min(128, KEYS - j * 128)
                        base = 7 * 512 + (j % 5) * 96
                        last = turn(PS[0:nk, base:base + 96], Z[:, b % 2, j * 128:j * 128 + nk], ident[0:96, 0:96])
                    last.then_inc(spt_ps, 1)
                pe.wait_ge(spt_ev, 2 * b + 2)
                for p in range(NPG):
                    pe.wait_ge(in_v[p], 16 * (b + 1))
                if b >= 1:
                    pe.wait_ge(spv_ev, 4 * b)
                for j in range(NPG + 1):
                    for x in range(3):
                        v = (Vr[:, j, x * 256:(x + 1) * 256] if j < NPG
                             else V[0:NS, 4, x * 256:(x + 1) * 256])
                        p = PTs[:, j, 32 * x:32 * x + 32] if j < NPG else PTs[0:NS, 8, 32 * x:32 * x + 32]
                        last = mm(PS[32 * x:32 * x + 32, 6 * 512:6 * 512 + 256], p, v, start=(j == 0), stop=(j == NPG))
                last.then_inc(spv_ps, 1)

            def turn_result(b):
                pe.wait_ge(ys_ready, b + 1)
                for k in range(2):
                    last = turn(PS[:, 6 * 512 + 256 + 96 * k:6 * 512 + 352 + 96 * k], Ys[:, k * 128:(k + 1) * 128],
                                ident[0:96, 0:96])
                last.then_inc(yt_ps, 1)

            pe.wait_ge(mt_ev, 8)
            pe.wait_ge(in_sc, 16)
            for b in range(DB + 1):
                if b < DB:
                    sampled_scores(b)
                else:
                    turn_result(DB - 2)
                if b >= 1:
                    sampled_values(b - 1)
            turn_result(DB - 1)

            pe.wait_ge(spv_ev, 4 * DB)
            pe.wait_ge(rw_done, 1)
            for g in range(2):
                w_wait(pe, P_OUT + g)
                for t, (t0, nr) in enumerate(TILES):
                    n = g * 5 + t
                    if n >= 8:
                        pe.wait_ge(o_ev, n - 7)
                    for k in range(KT):
                        last = mm(PS[0:nr, (n % 8) * 512:(n % 8 + 1) * 512], mixT[:, k, t0:t0 + nr],
                                  wview(P_OUT + g)[:, k, :], start=(k == 0), stop=(k == KT - 1))
                    last.then_inc(o_ps, 1)
            pe.wait_ge(o_ev, 10)
            for i, (t0, nr) in enumerate(TILES):
                pe.wait_ge(x2s_ready, i + 1)
                if i >= 2:
                    pe.wait_ge(h2_ready, i - 1)
                base = (i % 2) * 1024
                for k in range(KT):
                    last = turn(PS[:, base + k * 128:base + k * 128 + nr], xs[0:nr, i, k * 128:(k + 1) * 128],
                                ident[0:nr, 0:nr])
                last.then_inc(h2_ps, 1)
            pe.wait_ge(h2_ready, 5)
            for f in range(32):
                w_wait(pe, P_UP + f // 4)
                if f >= 4:
                    pe.wait_ge(u_ev, f - 3)
                out = pair(f % 4)
                for k in range(KT):
                    for a in range(2):
                        last = mm(out[:, a, :], wview(P_UP + f // 4)[:, k, (f % 4) * 128:(f % 4 + 1) * 128],
                                  h2T[:, k, a * 288:(a + 1) * 288], start=(k == 0), stop=(k == KT - 1))
                last.then_inc(u_ps, 1)
            pe.wait_ge(u_sq, 32)
            for n in range(2):
                def down(g, k, t):
                    t0, nr = TILES[t]
                    bank = (5 * n + t) % 8
                    return mm(PS[0:nr, bank * 512:(bank + 1) * 512], uT[:, 8 * g + k, t0:t0 + nr],
                              wview(P_DN + 4 * n + g)[:, k, :], start=(g == 0 and k == 0), stop=(g == 3 and k == 7))
                for g in range(4):
                    w_wait(pe, P_DN + 4 * n + g)
                    for t in range(5):
                        if n == 1 and g == 0 and 5 + t >= 8:
                            pe.wait_ge(y_ready, 5 + t - 7)
                        for k in range(8):
                            last = down(g, k, t)
                        if g == 3:
                            last.then_inc(y_ps, 1)
                        elif t == 4:
                            last.then_inc(dn_used, 1)

        @block.scalar
        def _(act):
            steps = [0]

            def link(ins):
                steps[0] += 1
                ins.then_inc(a_step, 1)
                act.wait_ge(a_step, steps[0])

            f = nc.scalar.activation

            act.wait_ge(init, 1)
            for i, (t0, nr) in enumerate(TILES):
                act.wait_ge(in_x[i], 16)
                f(xs[0:nr, i, :], xin[0:nr, i, :], ACT.Square, accum_out=ssq[0:nr, i:i + 1]).then_inc(squares, 1)
            act.wait_ge(squares, 5)
            f(rstd, ssq, ACT.Sqrt, scale=1.0 / D, bias=eps).then_inc(std_ready, 1)

            for m in range(8):
                act.wait_ge(p_ps, m + 1)
                f(halves(pT[:, m, :]), pair(m % 4), ACT.Copy).then_inc(p_ready, 1)

            def take(g):
                for t, (t0, nr) in enumerate(TILES):
                    r = g * 5 + t
                    act.wait_ge(qkv_ps, r + 1)
                    src = PS[0:nr, (r % 4) * 512:(r % 4) * 512 + QC]
                    if g >= 4:
                        if g == 5:
                            f(logf[0:nr, 4 * t:4 * t + 4], PS[0:nr, (r % 4) * 512 + QC:(r % 4) * 512 + QC + 4], ACT.Copy)
                        f(V[0:nr, t, (g - 4) * QC:(g - 3) * QC], src, ACT.Copy).then_inc(qkv_ev, 1)
                        continue
                    if g >= 2 and t == 0:
                        act.wait_ge(tr_ps, 5 * (g - 1))
                    f(ring[0:nr, g % 2, t, :], src, ACT.Copy).then_inc(qkv_ev, 1)
                    if r >= 3:
                        act.wait_ge(sq_used, r - 2)
                    act.wait_ge(qkv_ev, r + 1)
                    nh = (6, 2)[g % 2]
                    f(sqtmp[0:nr, r % 3, 0:nh * HD], ring[0:nr, g % 2, t, 0:nh * HD], ACT.Square).then_inc(sq_ready, 1)
                if g < 4:
                    act.wait_ge(sq_used, 5 * (g + 1))
                    f(qrs, qss, ACT.Sqrt, scale=1.0 / HD, bias=eps).then_inc(qstd_ready, 1)

            take(0)
            act.wait_ge(xm_ready, 1)
            f(xm[0:64, 6, :], xm[0:64, 6, :], ACT.Tanh).then_inc(lact, 1)
            f(xm[:, 7, :], xm[:, 7, :], ACT.Sigmoid).then_inc(lact, 1)
            take(1)
            for j in range(6):
                act.wait_ge(lora_ps, j + 1)
                dst = halves(slot((8, 9, 10)[j // 2])[:, j % 2, :])
                if j < 4:
                    c = (C_W0, C_A0)[j // 2] + j % 2
                    f(dst, pair(2 + j % 2), ACT.Sigmoid, bias=prm[:, c:c + 1]).then_inc(lora_ev, 1)
                else:
                    f(dst, pair(2 + j % 2), ACT.Copy).then_inc(lora_ev, 1)
            take(2)
            act.wait_ge(hs_ev, 2)
            f(slot(12), slot(12), ACT.Sqrt).then_inc(kkstd_ready, 1)
            act.wait_ge(exp_in, 1)
            for dst, src, sign in ((1, 1, 1.0), (2, 0, 1.0), (3, 0, -1.0), (7, 7, 1.0)):
                f(slot(dst), slot(src), ACT.Exp, scale=sign).then_inc(exp_out, 1)
            take(3)
            take(4)
            take(5)
            act.wait_ge(logf_in, 1)
            nc.scalar.preload_act_table_set("natural_log_exp_and_others")
            link(f(ftmp, ftmp, ACT.Exp))
            f(ftmp, ftmp, ACT.Ln, bias=1.0).then_inc(logf_a, 1)

            n_sb = [0]

            def attend(i):
                u = i - 6
                if 0 <= u < NU:
                    nk = (UNITS[u][0] + 1) * 128
                    act.wait_ge(pt_ps, u + 1)
                    if u >= 2:
                        act.wait_ge(pv_ps, u - 1)
                    f(PTp[:, u % 2, 0:nk], PS[:, 6 * 512:6 * 512 + nk], ACT.Copy).then_inc(pt_ev, 1)
                if i >= 20 and (i - 20) % 12 == 0:
                    qt = (i - 20) // 12
                    for n in range(2):
                        act.wait_ge(mt_ps, 2 * qt + n + 1)
                        f(mixT[:, 2 + 3 * n:5 + 3 * n, qt * 128:(qt + 1) * 128],
                          PS[:, 7 * 512:7 * 512 + 384].rearrange("p (j t) -> p j t", j=3), ACT.Copy).then_inc(mt_ev, 1)
                u = i - 4
                if 0 <= u < NU:
                    nk = (UNITS[u][0] + 1) * 128
                    bias = nmax[:, u % 8:u % 8 + 1]
                    x = Pp[u % NP_][:, 0:nk]
                    if is_sb(u):
                        n_sb[0] += 1
                        act.wait_ge(sb_in, n_sb[0])
                        f(x, x, ACT.Exp, bias=bias).then_inc(p_out, 1)
                    else:
                        act.wait_ge(a_in, u + 1)
                        f(x, x, ACT.Exp, bias=bias, accum_out=rsum[:, u % 8:u % 8 + 1]).then_inc(p_out, 1)
                u = i - 2
                if is_sb(u):
                    t1 = T1p[:, u % 2, 0:(UNITS[u][0] + 1) * 128]
                    act.wait_ge(a_in, u + 1)
                    link(f(t1, t1, ACT.Exp))
                    f(t1, t1, ACT.Ln, bias=1.0).then_inc(a_mid, 1)

            for what, i in ORDER:
                if what == "A":
                    attend(i)
                elif (what, i) == ("L", 2):
                    for h in range(4):
                        act.wait_ge(cb_ps, h + 1)
                        f(cb[:, h, :], PS[:, (4 + h) * 512:(5 + h) * 512], ACT.Copy).then_inc(cb_ready, 1)
                elif (what, i) == ("G", 0):
                    act.wait_ge(c_ev, len(STEPS))
                    f(slot(3), slot(3), ACT.Sqrt, bias=gneps).then_inc(gnstd_ready, 1)
                    nc.scalar.preload_act_table_set("natural_log_exp_and_others")

            def take_pages(b, pages):
                if b >= DB:
                    return
                for p in pages:
                    n = b * NPG + p
                    g = n // 2
                    if g >= 2 and p % 2 == 0:
                        act.wait_ge(sg_ps, g - 1)
                    for q in range(2):
                        m = 2 * n + q
                        act.wait_ge(kt_ps, m + 1)
                        base = (3 + m % 3) * 512
                        f(KTb[:, g % 2, 3 * q:3 * q + 3, (p % 2) * 128:(p % 2 + 1) * 128],
                          PS[:, base:base + 384].rearrange("p (c k) -> p c k", c=3), ACT.Copy).then_inc(kt_ev, 1)

            def scale_result(b):
                act.wait_ge(spv_ps, b + 1)
                if b >= 1:
                    act.wait_ge(yt_ps, b)
                f(Ys, PS[0:96, 6 * 512:6 * 512 + 256], ACT.Copy, scale=rinv[0:96, b % 2:b % 2 + 1]).then_inc(ys_ready, 1)

            def take_values(b):
                act.wait_ge(yt_ps, b + 1)
                c0 = SEQ + b * DT
                for k in range(2):
                    src = PS[:, 6 * 512 + 256 + 96 * k:6 * 512 + 352 + 96 * k].rearrange("p (x h q) -> p x h q", x=3, h=4)
                    for hf in range(2):
                        rows = slice(64 * hf, 64 * hf + 64)
                        f(mixT[rows, 2 + k:8:2, c0:c0 + DT], src[rows, :, 2 * k + hf, :], ACT.Copy).then_inc(spv_ev, 1)

            take_pages(0, range(NPG))
            for b in range(DB):
                z = Z[:, b % 2, :]
                act.wait_ge(ss_ps, b + 1)
                if b >= 2:
                    act.wait_ge(spt_ps, 2 * (b - 1))
                f(z[:, 0:PAST], PS[0:96, 0:PAST], ACT.Copy).then_inc(z_old, 1)
                act.wait_ge(z_abs, b + 1)
                link(f(T1[64:96, :], T1[64:96, :], ACT.Exp))
                f(T1[64:96, :], T1[64:96, :], ACT.Ln, bias=1.0).then_inc(z_ln, 1)
                if b >= 1:
                    scale_result(b - 1)
                take_pages(b + 1, range(0, 2))
                if b >= 1:
                    take_values(b - 1)
                take_pages(b + 1, range(2, 4))
                act.wait_ge(z_max, b + 1)
                f(z[0:64], z[0:64], ACT.Exp, bias=nmax[0:64, 0:1], accum_out=rsum[0:64, 0:1]).then_inc(z_exp, 1)
                take_pages(b + 1, range(4, 6))
                act.wait_ge(z_sb, b + 1)
                f(z[64:96], T1[64:96, :], ACT.Exp, bias=nmax[64:96, 0:1]).then_inc(z_exp, 1)
                take_pages(b + 1, range(6, NPG))
            scale_result(DB - 1)
            take_values(DB - 1)

            for i, (t0, nr) in enumerate(TILES):
                act.wait_ge(o_ev, 6 + i)
                f(xs[0:nr, i, :], x2[0:nr, i, :], ACT.Square, accum_out=ssq[0:nr, i:i + 1]).then_inc(x2_ssq, 1)
                act.wait_ge(x2_ssq, i + 1)
                f(rstd[:, i:i + 1], ssq[:, i:i + 1], ACT.Sqrt, scale=1.0 / D, bias=eps).then_inc(x2_std, 1)
            for n in range(32):
                act.wait_ge(u_ps, n + 1)
                f(halves(uT[:, n, :]), pair(n % 4), ACT.Relu).then_inc(u_ev, 1)

        @block.vector
        def _(dve):
            steps = [0]

            def link(ins):
                steps[0] += 1
                ins.then_inc(v_step, 1)
                dve.wait_ge(v_step, steps[0])

            tt, ts, stt = nc.vector.tensor_tensor, nc.vector.tensor_scalar, nc.vector.scalar_tensor_tensor
            copy, red, recip = nc.vector.tensor_copy, nc.vector.tensor_reduce, nc.vector.reciprocal
            MUL, ADD, SUB, MAX, MIN = ALU.mult, ALU.add, ALU.subtract, ALU.max, ALU.min

            def col(c):
                return prm[:, c:c + 1]

            link(nc.vector.memset(small[:, 0:128], 0.0))
            link(nc.vector.memset(small[:, 16:76], 1.0))
            link(nc.vector.memset(eps, RMS_EPS))
            link(nc.vector.memset(onec, 1.0))
            nc.vector.memset(gneps, GN_EPS).then_inc(init, 1)
            dve.wait_ge(in_const, 16 * 4)
            dve.wait_ge(std_ready, 1)
            link(recip(rstd, rstd))
            for i, (t0, nr) in enumerate(TILES):
                ts(xs[0:nr, i, :], xin[0:nr, i, :], rstd[0:nr, i:i + 1], None, MUL).then_inc(xs_ready, 1)

            def take_turned(i, dst, g0, done):
                t0, nr = TILES[i]
                base = (i % 2) * 1024
                tt(dst[:, :, t0:t0 + nr], PS[:, base:base + 1024].rearrange("p (k t) -> p k t", k=8)[:, :, 0:nr],
                   prm[:, g0:g0 + 8].unsqueeze(2).to_broadcast([128, 8, nr]), MUL).then_inc(done, 1)

            for i in range(5):
                dve.wait_ge(xT_ps, i + 1)
                take_turned(i, hT, C_AN, hT_ready)
            ts(omka, prm[:, C_KA:C_KA + 2], -1.0, 1.0, MUL, ADD).then_inc(v_step, 1)
            steps[0] += 1
            link(ts(gq, prm[:, C_QN:C_QN + 6], HD ** -0.5, None, MUL))

            dve.wait_ge(p_ready, 8)
            tt(xm[:, :, 1:SEQ], pT[:, :, 0:SEQ - 1], pT[:, :, 1:SEQ], SUB).then_inc(v_step, 1)
            ts(xm[:, :, 0:1], pT[:, :, 0:1], -1.0, None, MUL).then_inc(v_step, 1)
            steps[0] += 2
            for m in range(8):
                xs4 = xm[:, m, SEQ:].rearrange("p (b t) -> p b t", t=DT)
                ps4 = pT[:, m, SEQ:].rearrange("p (b t) -> p b t", t=DT)
                tt(xs4[:, :, 1:DT], ps4[:, :, 0:DT - 1], ps4[:, :, 1:DT], SUB).then_inc(v_step, 1)
                tt(xs4[:, :, 0:1], shift0[:, m, :].unsqueeze(2), ps4[:, :, 0:1], SUB).then_inc(v_step, 1)
                steps[0] += 2
            dve.wait_ge(v_step, steps[0])
            for m in range(8):
                ins = stt(xm[:, m, :], xm[:, m, :], col(C_MU + m), pT[:, m, :], MUL, ADD)
                if m < 7:
                    ins.then_inc(v_step, 1)
                    steps[0] += 1
            ins.then_inc(xm_ready, 1)
            dve.wait_ge(xm_ready, 1)
            dve.wait_ge(v_step, steps[0])
            dve.wait_ge(shift_ps, 1)
            copy(shift_sb, PS[0:9, 2048:3072]).then_inc(shift_ev, 1)
            link(nc.vector.memset(reset, 1.0))
            link(nc.vector.memset(reset[:, 0:SEQ:CH], 0.0))
            link(nc.vector.memset(reset[:, SEQ:T:DT], 0.0))

            def norm_sums(g):
                nh = (6, 2)[g % 2]
                if g:
                    dve.wait_ge(qstd_ready, g)
                for t, (t0, nr) in enumerate(TILES):
                    r = g * 5 + t
                    dve.wait_ge(sq_ready, r + 1)
                    red(qss[0:nr, t, 0:nh], sqtmp[0:nr, r % 3, 0:nh * HD].rearrange("p (h c) -> p h c", c=HD),
                        AX.X, ADD).then_inc(sq_used, 1)

            def norm_scale(g):
                nh = (6, 2)[g % 2]
                dve.wait_ge(qstd_ready, g + 1)
                link(recip(qrs, qrs))
                for t, (t0, nr) in enumerate(TILES):
                    x = ring[0:nr, g % 2, t, 0:nh * HD]
                    x3 = x.rearrange("p (h c) -> p h c", c=HD)
                    ins = tt(x3, x3, qrs[0:nr, t, 0:nh].unsqueeze(2).to_broadcast([nr, nh, HD]), MUL)
                    if g >= 2:
                        link(ins)
                        if g == 2 and t == 0:
                            dve.wait_ge(in_kn, 16)
                        ins = tt(x, x, knorm[0:nr, (g - 2) * QC:(g - 2) * QC + nh * HD], MUL)
                    ins.then_inc(qk_normed, 1)

            def take_qk(g):
                for t, (t0, nr) in enumerate(TILES):
                    r = g * 5 + t
                    dve.wait_ge(tr_ps, r + 1)
                    src = PS[:, (6 + r % 2) * 512:(6 + r % 2) * 512 + QC].rearrange("p (j t) -> p j t", j=3)[:, :, 0:nr]
                    c = 3 * (g % 2)
                    if g < 2:
                        ins = tt(qT[:, c:c + 3, t0:t0 + nr], src,
                                 gq[:, c:c + 3].unsqueeze(2).to_broadcast([128, 3, nr]), MUL)
                    else:
                        ins = copy(kT[:, c:c + 3, t0:t0 + nr], src)
                    ins.then_inc(tr_ev, 1)

            norm_sums(0)
            norm_scale(0)
            norm_sums(1)
            norm_scale(1)

            dve.wait_ge(lora_ev, 6)
            link(ts(slot(8), slot(8), DECAY, None, MUL))
            for a in range(2):
                link(nc.vector.tensor_tensor_scan(slot(0)[:, a, :], reset, slot(8)[:, a, :], 0.0, MUL, ADD))
            for a in range(2):
                link(ts(slot(11)[:, a, :], slot(5)[:, a, :], col(C_KK + a), None, MUL))
            tt(slot(12), slot(11), slot(11), MUL).then_inc(kksq_ready, 1)
            dve.wait_ge(shift_out, 32)
            for a in range(2):
                link(ts(slot(13)[:, a, :], slot(9)[:, a, :], col(C_KA + a), omka[:, a:a + 1], MUL, ADD))
            link(tt(slot(5), slot(5), slot(13), MUL))
            link(tt(slot(13), slot(4), slot(5), MUL))
            for a in range(2):
                ins = ts(slot(13)[:, a, :], slot(13)[:, a, :], col(C_RK + a), None, MUL)
                if a == 0:
                    link(ins)
            ins.then_inc(bonus_in, 1)
            take_qk(0)
            norm_sums(2)
            for a in range(2):
                dve.wait_ge(hs_ps, a + 1)
                if a == 0:
                    dve.wait_ge(kksq_ready, 1)
                ts(halves(slot(12)[:, a, :]), pair(2 + a), 1e-24, None, MAX).then_inc(hs_ev, 1)
            for a in range(2):
                dve.wait_ge(hs_ps, 3 + a)
                tt(halves(slot(13)[:, a, :]), pair(2 + a), halves(slot(6)[:, a, :]), MUL).then_inc(hs_ev, 1)
            link(tt(slot(1), slot(0), slot(8), SUB))
            for a in range(2):
                for s, n, w in ((slot(0)[:, a, 0:SEQ], 8, CH), (slot(0)[:, a, SEQ:T], 8, DT)):
                    lo = 0 if w == CH else SEQ
                    x = s.rearrange("p (c s) -> p c s", s=w)
                    y = slot(7)[:, a, lo:lo + n * w].rearrange("p (c s) -> p c s", s=w)
                    ins = tt(y, x[:, :, w - 1:w].to_broadcast([128, n, w]), x, SUB)
                    if a == 0 or w == CH:
                        link(ins)
            ins.then_inc(exp_in, 1)
            dve.wait_ge(kkstd_ready, 1)
            link(recip(slot(12), slot(12)))
            link(tt(slot(11), slot(11), slot(12), MUL))
            norm_scale(2)
            take_qk(1)
            dve.wait_ge(exp_out, 4)
            link(copy(pc[:, :, 0:8], slot(2)[:, :, CH - 1:SEQ:CH]))
            link(copy(pc[:, :, 8:16], slot(2)[:, :, SEQ + DT - 1:T:DT]))
            link(tt(slot(1), slot(1), slot(11), MUL))
            link(tt(slot(4), slot(4), slot(2), MUL))
            link(tt(slot(9), slot(9), slot(11), MUL))
            link(tt(slot(8), slot(9), slot(3), MUL))
            link(tt(slot(3), slot(5), slot(3), MUL))
            link(tt(slot(9), slot(9), slot(7), MUL))
            tt(slot(5), slot(5), slot(7), MUL).then_inc(ops_ready, 1)
            norm_sums(3)
            take_qk(2)
            norm_scale(3)
            take_qk(3)
            def log_sums(n):
                if n == 0:
                    dve.wait_ge(qkv_ev, 30)
                    lf3 = logf.rearrange("p (t h) -> p t h", h=4)
                    link(tt(lf3, lf3, prm[:, C_BF:C_BF + 4].unsqueeze(1).to_broadcast([128, 5, 4]), ADD))
                    ts(ftmp, logf, -1.0, SP_MAX, MUL, MIN).then_inc(logf_in, 1)
                elif n == 1:
                    dve.wait_ge(logf_a, 1)
                    stt(logf, ftmp, -1.0, logf, MUL, MIN).then_inc(logf_ready, 1)
                    dve.wait_ge(logf_ready, 1)
                    copy(lfx.rearrange("p (b h) -> p b h", b=DB),
                         logf[0:NS, 16:20].unsqueeze(1).to_broadcast([NS, DB, 4])).then_inc(lfx_ready, 1)
                else:
                    dve.wait_ge(lt_ps, 1)
                    dve.wait_ge(in_s0, 16)
                    link(copy(cT, PS[0:4, 2048:2048 + SEQ]))
                    nc.vector.tensor_tensor_scan(cT, onec[0:4].to_broadcast([4, SEQ]), cT, 0.0, MUL, ADD).then_inc(cT_ready, 1)
                    dve.wait_ge(in_pc, 16)
                    link(tt(Call[:, PAST:KEYS], PS[0:32, 2560:2560 + NS], own[0:32], MUL))
                    nc.vector.memset(T2p[:, 0:1], 0.0).then_inc(lfn_ready, 1)

            dve.wait_ge(in_rc, 16)

            def take(kind, a):
                n = AT[kind, a]
                dve.wait_ge(c_ps, n + 1)
                return PS[:, (n % 2) * 1024:(n % 2) * 1024 + T]

            def r3(ap):
                return ap.rearrange("p (c s) -> p c s", s=CH)

            def mask64(c0, n=NCH):
                return rc[:, c0:c0 + 64].unsqueeze(1).to_broadcast([128, n, 64])

            id64 = cst[:, K_ID64:K_ID64 + 64].unsqueeze(1).to_broadcast([128, NCH, 64])
            def rwkv_steps():
                for kind, dst, m in (("LT", 0, R_SU), ("L", 2, None), ("ArbT", 11, R_IU), ("LkT", 7, R_SU), ("ArkT", 12, R_IU)):
                    for a in range(2):
                        src = take(kind, a)
                        if kind == "L":
                            link(tt(chunked(dst)[:, a], r3(src), mask64(R_L1), MUL))
                            tt(chunked(dst)[:, a], id64, chunked(dst)[:, a], SUB).then_inc(c_ev, 1)
                            yield
                        else:
                            tt(slot(dst)[:, a, :], src, rc[:, m:m + T], MUL).then_inc(c_ev, 1)
                            yield
                def level_mask(lev, a):
                    tt(chunked(3)[:, a], chunked(0)[:, a], mask64(R_LEV + 64 * lev), MUL).then_inc(ltm_ready, 1)

                for kind, dst in (("Vt", 14), ("KQt", 15), ("BEt", 17), ("KEt", 18)):
                    for a in range(2):
                        copy(slot(dst)[:, a, :], take(kind, a)).then_inc(c_ev, 1)
                        if kind in ("Vt", "KQt"):
                            if kind == "Vt":
                                link(tt(chunked(8)[:, a], chunked(0)[:, a], mask64(R_L1T), MUL))
                                link(tt(chunked(8)[:, a], id64, chunked(8)[:, a], SUB))
                            else:
                                level_mask(0, a)
                        yield
                dve.wait_ge(c_ev, AT["KEt", 1] + 1)
                for lev in range(5):
                    for a in range(2):
                        copy(slot(5)[:, a, :], take(f"W{lev}", a)).then_inc(c_ev, 1)
                        if lev < 4:
                            level_mask(lev + 1, a)
                        yield
                    for k, x in ((("dX", 2), ("dXT", 8)) if lev < 4 else (("dXT", 8),)):
                        for a in range(2):
                            src = take(f"{k}{lev}", a)
                            if x == 8 and lev < 4 or x == 2:
                                dve.wait_ge(c_ps, AT[f"dXT{lev}", a] + 1 if x == 8 else AT[f"dX{lev}", a] + 1)
                            tt(slot(x)[:, a, :], slot(x)[:, a, :], src, SUB).then_inc(c_ev, 1)
                            yield
                dve.wait_ge(c_ev, AT["dXT4", 1] + 1)
                for a in range(2):
                    copy(slot(9)[:, a, :], take("T1", a)).then_inc(c_ev, 1)
                    yield
                for kind, dst in (("HT", 0), ("H", 1), ("G", 19)):
                    for a in range(2):
                        ts(slot(dst)[:, a, :], take(kind, a), -1.0, None, MUL).then_inc(c_ev, 1)
                        yield
                for a in range(2):
                    if a == 0:
                        dve.wait_ge(c_ev, AT["G", 1] + 1)
                    link(tt(chunked(2)[:, a, 0:8], cst[:, K_ID64:K_ID64 + 64].unsqueeze(1).to_broadcast([128, 8, 64]),
                            pc[:, a, 0:8].unsqueeze(2).to_broadcast([128, 8, 64]), MUL))
                    src = take("MT", a)
                    tt(chunked(2)[:, a, 0:8], chunked(2)[:, a, 0:8], r3(src)[:, 0:8], ADD).then_inc(c_ev, 1)
                    dve.wait_ge(in_s0, 16)
                    tt(hexp[:, a], chunked(0)[:, a, 8:9, :].to_broadcast([128, DB, 64]),
                       rc[:, R_BM:R_BM + 512].rearrange("p (b t) -> p b t", b=DB), MUL).then_inc(masked_ready, 1)
                    yield
                for a in range(2):
                    copy(slot(3)[:, a, 0:SEQ], take("N", a)[:, 0:SEQ]).then_inc(c_ev, 1)
                    if a == 1:
                        dve.wait_ge(c_ev, AT["N", 1] + 1)
                        copy(chunked(5)[:, :, 1, :], chunked(3)[:, :, 0, :]).then_inc(s1_ready, 1)
                    yield
                for c in range(1, 8):
                    n = AT[f"seq{c}", 0]
                    dve.wait_ge(c_ps, n + 1)
                    src = PS[:, (n % 2) * 1024:(n % 2) * 1024 + 128].rearrange("p (a i) -> p a i", a=2)
                    dst = chunked(5)[:, :, c + 1, :] if c < 7 else sfin
                    tt(dst, src, chunked(3)[:, :, c, :], ADD).then_inc(c_ev, 1)
                    yield
                for a in range(2):
                    src = take("U", a)
                    link(copy(slot(9)[:, a, 0:CH], slot(19)[:, a, 0:CH]))
                    tt(slot(9)[:, a, CH:T], src[:, CH:T], slot(19)[:, a, CH:T], ADD).then_inc(c_ev, 1)
                    yield
                for a in range(2):
                    copy(slot(6)[:, a, :], take("Y", a)).then_inc(c_ev, 1)
                    if a == 1:
                        for a2 in range(2):
                            bm = prm[:, C_BM:C_BM + DB].unsqueeze(2).to_broadcast([128, DB, 64])
                            link(tt(uexp[:, a2], chunked(9)[:, a2, 8:9, :].to_broadcast([128, DB, 64]), bm, MUL))
                            tt(hexp[:, a2], chunked(14)[:, a2, 8:9, :].to_broadcast([128, DB, 64]), bm,
                               MUL).then_inc(masked_ready, 1)
                    yield
                for a in range(2):
                    link(tt(S0[:, a], S0[:, a], pc[:, a, 8:16].unsqueeze(2).to_broadcast([128, DB, 64]), MUL))
                    src = take("SS", a)
                    tt(S0[:, a], S0[:, a], src[:, 0:512].rearrange("p (b i) -> p b i", b=DB), ADD).then_inc(c_ev, 1)
                    yield
                for a in range(2):
                    dve.wait_ge(c_ps, AT["GM", a] + 1)
                    y = halves(slot(6)[:, a, :])
                    link(stt(y, pair(AT["GM", a] % 2), -1.0 / HD, y, MUL, ADD))
                    tt(slot(3)[:, a, :], slot(6)[:, a, :], slot(6)[:, a, :], MUL).then_inc(c_ev, 1)
                    yield
                for a in range(2):
                    dve.wait_ge(c_ps, AT["GV", a] + 1)
                    ts(halves(slot(3)[:, a, :]), pair(AT["GV", a] % 2), 1.0 / HD, None, MUL).then_inc(c_ev, 1)
                    yield

            def rwkv_end():
                dve.wait_ge(gnstd_ready, 1)
                link(recip(slot(3), slot(3)))
                link(tt(slot(6), slot(6), slot(3), MUL))
                for a in range(2):
                    link(ts(slot(6)[:, a, :], slot(6)[:, a, :], col(C_GW + a), col(C_GB + a), MUL, ADD))
                link(tt(slot(6), slot(6), slot(13), ADD))
                tt(mixT[:, 0:2, :], slot(6), slot(10), MUL).then_inc(rw_done, 1)

            n_mid = [0]

            def front(u):
                qt, h = UNITS[u]
                nk = (qt + 1) * 128
                z = PS[:, (4 + u % 2) * 512:(4 + u % 2) * 512 + nk]
                x = Pp[u % NP_][:, 0:nk]
                dve.wait_ge(s_ps, u + 1)
                if u >= NP_:
                    dve.wait_ge(pt_ps, u - NP_ + 1)
                if h < 4:
                    tt(x, z, cb[:, h, 0:nk], ADD).then_inc(s_ev, 1)
                else:
                    copy(x, z).then_inc(s_ev, 1)
                dve.wait_ge(s_ev, u + 1)
                m = K_CAU if h < 8 else K_STR
                link(tt(x[:, nk - 128:nk], x[:, nk - 128:nk], cst[:, m:m + 128], ADD))
                if h < 8:
                    red(nmax[:, u % 8:u % 8 + 1], x, AX.X, MAX, negate=True).then_inc(a_in, 1)
                else:
                    ts(T1p[:, u % 2, 0:nk], x, SP_MAX, None, MIN).then_inc(a_in, 1)

            def mid(u):
                qt, h = UNITS[u]
                nk = (qt + 1) * 128
                x = Pp[u % NP_][:, 0:nk]
                t1 = T1p[:, u % 2, 0:nk]
                n_mid[0] += 1
                dve.wait_ge(a_mid, n_mid[0])
                link(tt(t1, x, t1, MAX))
                link(nc.vector.tensor_tensor_scan(T2p[:, 1:nk + 1], onec.to_broadcast([128, nk]), t1, 0.0, MUL, ADD))
                link(tt(x, x, T2p[:, 0:nk], ADD))
                ts(nmax[:, u % 8:u % 8 + 1], T2p[:, nk:nk + 1], -1.0, None, MUL).then_inc(sb_in, 1)

            def take_out(u):
                qt, h = UNITS[u]
                dve.wait_ge(pv_ps, u + 1)
                if h == 0 and qt >= 2:
                    dve.wait_ge(mt_ps, 2 * (qt - 1))
                src = PS[:, 7 * 512:7 * 512 + 64]
                dst = Ya[:, qt % 2, h * HD:(h + 1) * HD]
                if h < 8:
                    r = rinv[:, u % 8:u % 8 + 1]
                    link(recip(r, rsum[:, u % 8:u % 8 + 1]))
                    ts(dst, src, r, None, MUL).then_inc(pv_ev, 1)
                else:
                    copy(dst, src).then_inc(pv_ev, 1)

            rwkv = rwkv_steps()
            for what, i in ORDER:
                if what == "R":
                    next(rwkv)
                elif what == "L":
                    log_sums(i)
                elif (what, i) == ("G", 1):
                    rwkv_end()
                elif what == "A":
                    if is_sb(i - 3):
                        mid(i - 3)
                    if 0 <= i - 1 < NU:
                        front(i - 1)
                    if 0 <= i - 7 < NU:
                        take_out(i - 7)

            dve.wait_ge(mt_ps, 8)
            link(nc.vector.memset(qbd[:, :, :, :], 0.0))
            link(nc.vector.memset(T2[:, 0:1], 0.0))
            link(nc.vector.memset(rinv[64:96, 0:2], 1.0))
            dve.wait_ge(in_lf, 16 * DB * NPG)
            dve.wait_ge(in_sc, 16)
            nc.vector.tensor_tensor_scan(Call, onec[0:32].to_broadcast([32, KEYS]), Call, 0.0, MUL, ADD).then_inc(call_ready, 1)

            def spread_q(b):
                if b >= 2:
                    dve.wait_ge(ss_ps, b - 1)
                c0 = SEQ + b * DT
                for k in range(2):
                    for hf in range(2):
                        rows = slice(64 * hf, 64 * hf + 64)
                        q0 = 16 * k + 8 * hf
                        ins = copy(qbd[rows, b % 2, k:6:2, q0:q0 + 8], qT[rows, k:6:2, c0:c0 + DT])
                        if (k, hf) != (1, 1):
                            link(ins)
                ins.then_inc(qbd_ready, 1)

            def take_new(b):
                dve.wait_ge(ss_ps, b + 1)
                if b >= 2:
                    dve.wait_ge(spt_ps, 2 * (b - 1))
                tt(Z[:, b % 2, PAST:KEYS], PS[0:96, PAST:KEYS], rc[0:96, S_MASK + 64 * b:S_MASK + 64 * b + 64],
                   ADD).then_inc(z_new, 1)

            def sampled_softmax(b):
                z = Z[:, b % 2, :]
                dve.wait_ge(z_old, b + 1)
                dve.wait_ge(z_new, b + 1)
                if b:
                    dve.wait_ge(z_exp, 2 * b)
                ts(T1[64:96, :], z[64:96], SP_MAX, None, MIN).then_inc(z_abs, 1)
                m = slice(32, 64)
                old = z[m, 0:PAST].rearrange("p (n k) -> p n k", n=NBLK)
                link(red(gate[m], old, AX.X, ADD))
                link(red(gmin[m, 0:1], gate[m], AX.X, MIN))
                link(ts(gsel[m], gate[m], gmin[m, 0:1], None, ALU.is_equal))
                link(tt(gsel[m], gsel[m], rc[m, S_IOTA:S_IOTA + NBLK], MUL))
                link(red(gmin[m, 1:2], gsel[m], AX.X, MAX))
                link(ts(gsel[m], gsel[m], gmin[m, 1:2], NEG, ALU.is_equal, MUL))
                link(tt(old, old, gsel[m].unsqueeze(2).to_broadcast([32, NBLK, BLK]), ADD))
                red(nmax[0:64, 0:1], z[0:64], AX.X, MAX, negate=True).then_inc(z_max, 1)
                dve.wait_ge(z_ln, b + 1)
                s = slice(64, 96)
                link(tt(T1[s], z[s], T1[s], MAX))
                link(nc.vector.tensor_tensor_scan(T2[s, 1:KEYS + 1], onec[s].to_broadcast([32, KEYS]), T1[s], 0.0, MUL, ADD))
                link(tt(T1[s], z[s], T2[s, 0:KEYS], ADD))
                ts(nmax[s, 0:1], T2[s, KEYS:KEYS + 1], -1.0, None, MUL).then_inc(z_sb, 1)
                dve.wait_ge(z_exp, 2 * b + 2)
                if b >= 2:
                    dve.wait_ge(ys_ready, b - 1)
                recip(rinv[0:64, b % 2:b % 2 + 1], rsum[0:64, 0:1]).then_inc(pn_ready, 1)

            def take_turned_p(b):
                for jj in range(2):
                    dve.wait_ge(spt_ps, 2 * b + jj + 1)
                    if b and jj == 0:
                        dve.wait_ge(spv_ps, b)
                    if jj == 0:
                        copy(PTs[:, 0:5, :], PS[:, 7 * 512:7 * 512 + 480].rearrange("p (j r) -> p j r", j=5)).then_inc(spt_ev, 1)
                    else:
                        link(copy(PTs[:, 5:8, :], PS[:, 7 * 512:7 * 512 + 288].rearrange("p (j r) -> p j r", j=3)))
                        copy(PTs[0:NS, 8, :], PS[0:NS, 7 * 512 + 288:7 * 512 + 384]).then_inc(spt_ev, 1)

            spread_q(0)
            for b in range(DB + 1):
                if b + 1 < DB:
                    spread_q(b + 1)
                if b < DB:
                    take_new(b)
                if b >= 1:
                    take_turned_p(b - 1)
                if b < DB:
                    sampled_softmax(b)

            dve.wait_ge(in_resid, 16 * 5)
            for n in range(10):
                g, t = divmod(n, 5)
                t0, nr = TILES[t]
                dve.wait_ge(o_ps, n + 1)
                x = x2[0:nr, t, g * 512:(g + 1) * 512]
                tt(x, x, PS[0:nr, (n % 8) * 512:(n % 8 + 1) * 512], ADD).then_inc(o_ev, 1)
            for i, (t0, nr) in enumerate(TILES):
                dve.wait_ge(x2_std, i + 1)
                link(recip(rstd[:, i:i + 1], rstd[:, i:i + 1]))
                ts(xs[0:nr, i, :], x2[0:nr, i, :], rstd[0:nr, i:i + 1], None, MUL).then_inc(x2s_ready, 1)
                if i >= 1:
                    dve.wait_ge(h2_ps, i)
                    take_turned(i - 1, h2T, C_MN, h2_ready)
            dve.wait_ge(h2_ps, 5)
            take_turned(4, h2T, C_MN, h2_ready)
            for n in range(32):
                dve.wait_ge(u_ev, n + 1)
                tt(uT[:, n, :], uT[:, n, :], uT[:, n, :], MUL).then_inc(u_sq, 1)
            for n in range(10):
                g, t = divmod(n, 5)
                t0, nr = TILES[t]
                dve.wait_ge(y_ps, n + 1)
                x = x2[0:nr, t, g * 512:(g + 1) * 512]
                tt(x, x, PS[0:nr, (n % 8) * 512:(n % 8 + 1) * 512], ADD).then_inc(y_ready, 1)


def _channels(a, n):
    return np.ascontiguousarray(np.asarray(a).reshape(n, 128).T)


def kernel(**inputs):
    import concourse.bacc as bacc
    from concourse.bass_utils import run_bass_kernel_spmd

    v = {k: np.ascontiguousarray(a) for k, a in inputs.items()}
    cst, rc, sc, pcst = constants()
    prm = np.zeros((128, N_PRM), np.float32)
    for name, c, n in (("attn_norm", C_AN, 8), ("mlp_norm", C_MN, 8), ("rwkv_mu", C_MU, 8), ("rwkv_w0", C_W0, 2),
                       ("rwkv_a0", C_A0, 2), ("rwkv_k_k", C_KK, 2), ("rwkv_k_a", C_KA, 2), ("rwkv_r_k", C_RK, 2),
                       ("rwkv_gn_w", C_GW, 2), ("rwkv_gn_b", C_GB, 2), ("q_norm", C_QN, 4)):
        prm[:, c:c + n] = _channels(v[name], n)
    prm[:, C_QN + 4:C_QN + 6] = 1
    prm[:, C_BM:C_BM + DB] = (np.arange(128)[:, None] % 64 // DT == np.arange(DB)[None, :])
    prm[:, C_BF:C_BF + 4] = v["b_forget"]
    arrays = {n: v[n] for n in ("x_prompt", "x_sample", "cache_kv", "page_table", "w_in", "rwkv_g_up", "k_norm",
                                "w_out", "w_mlp_up", "w_mlp_down")}
    arrays["logf_t"] = np.ascontiguousarray(v["cache_logf"][0].transpose(0, 2, 1))
    arrays["lora_wa"] = np.concatenate([v["rwkv_w_up"][0], v["rwkv_a_up"][0]], axis=0)
    arrays["shift0"] = np.ascontiguousarray(v["state_shift"][0].reshape(DB, 8, 128).transpose(2, 1, 0).reshape(128, 64))
    arrays["s0"] = np.ascontiguousarray(v["state_wkv"][0].reshape(DB, 2, 2, HD, HD).transpose(2, 4, 1, 0, 3).reshape(128, 1024))
    arrays.update(cst=cst, rc=rc, sc=sc, pcst=pcst, prm=prm)
    arrays = {n: np.ascontiguousarray(a) for n, a in arrays.items()}
    outs = {"y_prompt": (SEQ, D), "y_sample": (NS, D), "kv_prompt": (SEQ, 2 * AW), "kv_sample": (NS, 2 * AW),
            "logf_prompt": (SEQ, 4), "logf_sample": (NS, 4), "wkv_prompt": (128, 128), "wkv_sample": (128, 1024),
            "shift_prompt": (1, N_RW), "shift_sample": (DB, N_RW)}

    nc = bacc.Bacc("TRN2", target_bir_lowering=False, num_devices=1)
    d = {n: nc.dram_tensor(f"in_{n}", a.shape, mybir.dt.from_np(a.dtype), kind="ExternalInput").ap()
         for n, a in arrays.items()}
    o = {n: nc.dram_tensor(f"out_{n}", s, F32, kind="ExternalOutput").ap() for n, s in outs.items()}
    build(nc, d, o)
    r = run_bass_kernel_spmd(nc, [{f"in_{n}": a for n, a in arrays.items()}], core_ids=[0]).results[0]
    g = {n: np.asarray(r[f"out_{n}"]) for n in outs}
    wkv_p = g["wkv_prompt"].reshape(2, HD, 2, HD).transpose(2, 0, 3, 1).reshape(1, 1, 4, HD, HD)
    wkv_s = g["wkv_sample"].reshape(2, HD, 2, DB, HD).transpose(3, 2, 0, 4, 1).reshape(1, DB, 4, HD, HD)
    return (g["y_prompt"].reshape(1, SEQ, D), g["y_sample"].reshape(DB, DT, D),
            g["kv_prompt"].reshape(1, 1, SEQ, 2, H_ATT, HD), g["kv_sample"].reshape(1, DB, DT, 2, H_ATT, HD),
            g["logf_prompt"].reshape(1, 1, SEQ, 4), g["logf_sample"].reshape(1, DB, DT, 4),
            np.ascontiguousarray(wkv_p), np.ascontiguousarray(wkv_s),
            g["shift_prompt"].reshape(1, 1, N_RW), g["shift_sample"].reshape(1, DB, N_RW))
```
